# Optimizing a Trainium2 kernel written in Bass

```python
import math
import jax, jax.numpy as jnp
from jax import lax
import numpy as np

D_MODEL = 1024
BATCH = 1
SEQ = 512
DEPTH = 2

MIX_W = 768
XATT_HEADS = 4
XATT_DH = 64
XATT_W = XATT_HEADS * XATT_DH
MEM_LEN = 256
CONV_K = 3
ML_HEADS = 6
ML_DH = MIX_W // ML_HEADS
CHUNK = 128
D_IN_CONV = 3 * MIX_W + XATT_W
D_IN_MLSTM = 4 * MIX_W + 2 * ML_HEADS + XATT_W
N_CONV = (DEPTH + 1) // 2
N_MLSTM = DEPTH // 2
N_EXPERTS = 32
N_GROUPS = 8
EXPERTS_PER_GROUP = N_EXPERTS // N_GROUPS
TOP_K = 2
D_FF = 512
MOE_BLOCK = 128
ALPHA = (2.0 * DEPTH) ** 0.25
BETA = (8.0 * DEPTH) ** -0.25
LN_EPS = 1e-5

kernel_name = "hybrid_conv_mlstm_xattn_moe_deepnorm"

def layer_norm(x, g, b):
    xf = x.astype(jnp.float32)
    mu = jnp.mean(xf, axis=-1, keepdims=True)
    var = jnp.mean(jnp.square(xf - mu), axis=-1, keepdims=True)
    return ((xf - mu) * lax.rsqrt(var + LN_EPS) * g + b).astype(x.dtype)

def conv_mixer(x, w_in, conv_w):
    proj = x @ w_in
    bg = proj[..., :MIX_W]
    cg = proj[..., MIX_W:2 * MIX_W]
    xin = proj[..., 2 * MIX_W:3 * MIX_W]
    q_mem = proj[..., 3 * MIX_W:]
    u = cg * xin
    seq = u.shape[1]
    up = jnp.pad(u, ((0, 0), (CONV_K - 1, 0), (0, 0)))
    c = (conv_w[0] * up[:, 0:seq] + conv_w[1] * up[:, 1:seq + 1] + conv_w[2] * up[:, 2:seq + 2])
    return bg * c, q_mem

def mlstm_cell(q, k, v, log_i, log_f):
    nb, nh, seq, dh = q.shape
    nc = seq // CHUNK
    q = q.reshape(nb, nh, nc, CHUNK, dh)
    k = k.reshape(nb, nh, nc, CHUNK, dh)
    v = v.reshape(nb, nh, nc, CHUNK, dh)
    log_i = log_i.reshape(nb, nh, nc, CHUNK)
    log_f = log_f.reshape(nb, nh, nc, CHUNK)
    b = jnp.cumsum(log_f, axis=-1)
    g = b[..., -1]
    a = g[..., None] - b + log_i

    def step(carry, inp):
        c_st, n_st, m_st = carry
        kc, vc, ac, gc = inp
        m_new = jnp.maximum(gc + m_st, ac.max(-1))
        decay = jnp.exp(gc + m_st - m_new)
        w = jnp.exp(ac - m_new[..., None])
        c_new = decay[..., None, None] * c_st + jnp.einsum('bhl,bhld,bhle->bhde', w, kc, vc)
        n_new = decay[..., None] * n_st + jnp.einsum('bhl,bhld->bhd', w, kc)
        return (c_new, n_new, m_new), (c_st, n_st, m_st)

    init = (jnp.zeros((nb, nh, dh, dh), jnp.float32),
            jnp.zeros((nb, nh, dh), jnp.float32),
            jnp.zeros((nb, nh), jnp.float32))
    xs = (jnp.moveaxis(k, 2, 0), jnp.moveaxis(v, 2, 0), jnp.moveaxis(a, 2, 0), jnp.moveaxis(g, 2, 0))
    _, (c_prev, n_prev, m_prev) = lax.scan(step, init, xs)
    c_prev = jnp.moveaxis(c_prev, 0, 2)
    n_prev = jnp.moveaxis(n_prev, 0, 2)
    m_prev = jnp.moveaxis(m_prev, 0, 2)

    causal = jnp.tril(jnp.ones((CHUNK, CHUNK), dtype=bool))
    d = jnp.where(causal, b[..., :, None] - b[..., None, :] + log_i[..., None, :], -jnp.inf)
    inter = b + m_prev[..., None]
    m_t = jnp.maximum(d.max(-1), inter)
    s = jnp.einsum('bhcld,bhcsd->bhcls', q, k) * jnp.exp(d - m_t[..., None])
    w_inter = jnp.exp(inter - m_t)
    num = (jnp.einsum('bhcls,bhcsd->bhcld', s, v)
           + w_inter[..., None] * jnp.einsum('bhcld,bhcde->bhcle', q, c_prev))
    den = s.sum(-1) + w_inter * jnp.einsum('bhcld,bhcd->bhcl', q, n_prev)
    h = num / jnp.maximum(jnp.abs(den), jnp.exp(-m_t))[..., None]
    return h.reshape(nb, nh, seq, dh)

def mlstm_mixer(x, w_in, gate_b, norm_g):
    nb, seq, _ = x.shape
    proj = x @ w_in
    o0 = 4 * MIX_W

    def heads(t):
        return t.reshape(nb, seq, ML_HEADS, ML_DH).transpose(0, 2, 1, 3).astype(jnp.float32)

    q = heads(proj[..., 0:MIX_W])
    k = heads(proj[..., MIX_W:2 * MIX_W]) * (ML_DH ** -0.5)
    v = heads(proj[..., 2 * MIX_W:3 * MIX_W])
    o_gate = proj[..., 3 * MIX_W:4 * MIX_W]
    log_i = (proj[..., o0:o0 + ML_HEADS] + gate_b[:ML_HEADS]).astype(jnp.float32).transpose(0, 2, 1)
    log_f = jax.nn.log_sigmoid((proj[..., o0 + ML_HEADS:o0 + 2 * ML_HEADS]
                                + gate_b[ML_HEADS:]).astype(jnp.float32)).transpose(0, 2, 1)
    q_mem = proj[..., o0 + 2 * ML_HEADS:]
    h = mlstm_cell(q, k, v, log_i, log_f)
    mu = jnp.mean(h, axis=-1, keepdims=True)
    var = jnp.mean(jnp.square(h - mu), axis=-1, keepdims=True)
    h = ((h - mu) * lax.rsqrt(var + LN_EPS)).transpose(0, 2, 1, 3).reshape(nb, seq, MIX_W)
    h = (h * norm_g).astype(x.dtype)
    return jax.nn.sigmoid(o_gate) * h, q_mem

def cross_attention(q_mem, mem, w_kv):
    nb, seq, _ = q_mem.shape
    kv = mem @ w_kv
    k = kv[..., :XATT_W].reshape(nb, -1, XATT_HEADS, XATT_DH)
    v = kv[..., XATT_W:].reshape(nb, -1, XATT_HEADS, XATT_DH)
    q = q_mem.reshape(nb, seq, XATT_HEADS, XATT_DH)
    s = jnp.einsum('bshd,bmhd->bhsm', q, k).astype(jnp.float32) * (XATT_DH ** -0.5)
    p = jax.nn.softmax(s, axis=-1).astype(v.dtype)
    return jnp.einsum('bhsm,bmhd->bshd', p, v).reshape(nb, seq, XATT_W)

def grouped_moe(x2, router_w, router_b, w_gate, w_up, w_down):
    n_tok, d = x2.shape
    scores = jax.nn.sigmoid((x2 @ router_w).astype(jnp.float32))
    sel = (scores + router_b).reshape(n_tok, N_GROUPS, EXPERTS_PER_GROUP)
    group_score = lax.top_k(sel, TOP_K)[0].sum(-1)
    _, g_idx = lax.top_k(group_score, 1)
    in_group = jnp.take_along_axis(sel, g_idx[:, :, None], axis=1)[:, 0]
    _, local = lax.top_k(in_group, TOP_K)
    expert = g_idx * EXPERTS_PER_GROUP + local
    gates = jnp.take_along_axis(scores, expert, axis=1)
    gates = gates / gates.sum(-1, keepdims=True)

    n_asg = n_tok * TOP_K
    e_flat = expert.reshape(n_asg)
    tok_flat = jnp.repeat(jnp.arange(n_tok, dtype=jnp.int32), TOP_K)
    g_flat = gates.reshape(n_asg)
    counts = jax.ops.segment_sum(jnp.ones((n_asg,), jnp.int32), e_flat, num_segments=N_EXPERTS)
    padded = (counts + MOE_BLOCK - 1) // MOE_BLOCK * MOE_BLOCK
    pad_end = jnp.cumsum(padded)
    pad_start = pad_end - padded
    start = jnp.cumsum(counts) - counts
    order = jnp.argsort(e_flat)
    e_sorted = e_flat[order]
    dest = pad_start[e_sorted] + (jnp.arange(n_asg, dtype=jnp.int32) - start[e_sorted])
    n_rows = ((n_asg + MOE_BLOCK - 1) // MOE_BLOCK + N_EXPERTS) * MOE_BLOCK
    n_blocks = n_rows // MOE_BLOCK
    tok_buf = jnp.zeros((n_rows,), jnp.int32).at[dest].set(tok_flat[order])
    gate_buf = jnp.zeros((n_rows,), x2.dtype).at[dest].set(g_flat[order].astype(x2.dtype))
    block_start = jnp.arange(n_blocks, dtype=jnp.int32) * MOE_BLOCK
    block_expert = jnp.clip(jnp.searchsorted(pad_end, block_start, side='right'), 0, N_EXPERTS - 1)
    xb = x2[tok_buf].reshape(n_blocks, MOE_BLOCK, d)

    def expert_block(args):
        xblk, e = args
        h = jax.nn.silu(xblk @ w_gate[e]) * (xblk @ w_up[e])
        return h @ w_down[e]

    yb = lax.map(expert_block, (xb, block_expert)).reshape(n_rows, d)
    return jnp.zeros_like(x2).at[tok_buf].add(yb * gate_buf[:, None])

def setup_inputs(seed: int = 0) -> dict:
    key = jax.random.key(seed)
    ks = jax.random.split(key, 20)
    f32 = jnp.float32
    nrm = lambda k, s, sc: jax.random.normal(k, s, f32) * sc
    gate_i = nrm(ks[5], (N_MLSTM, ML_HEADS), 0.1)
    gate_f = jax.random.uniform(ks[6], (N_MLSTM, ML_HEADS), f32, 3.0, 6.0)
    return {
        "x": nrm(ks[0], (BATCH, SEQ, D_MODEL), 1.0),
        "mem": nrm(ks[1], (BATCH, MEM_LEN, D_MODEL), 1.0),
        "conv_w_in": nrm(ks[2], (N_CONV, D_MODEL, D_IN_CONV), D_MODEL ** -0.5),
        "conv_w": nrm(ks[3], (N_CONV, CONV_K, MIX_W), CONV_K ** -0.5),
        "mlstm_w_in": nrm(ks[4], (N_MLSTM, D_MODEL, D_IN_MLSTM), D_MODEL ** -0.5),
        "mlstm_gate_b": jnp.concatenate([gate_i, gate_f], axis=-1),
        "mlstm_norm_g": 1.0 + nrm(ks[7], (N_MLSTM, MIX_W), 0.02),
        "w_kv_mem": nrm(ks[8], (DEPTH, D_MODEL, 2 * XATT_W), D_MODEL ** -0.5),
        "w_out": nrm(ks[9], (DEPTH, MIX_W + XATT_W, D_MODEL), (MIX_W + XATT_W) ** -0.5 * BETA),
        "ln1_g": 1.0 + nrm(ks[10], (DEPTH, D_MODEL), 0.02),
        "ln1_b": nrm(ks[11], (DEPTH, D_MODEL), 0.02),
        "ln2_g": 1.0 + nrm(ks[12], (DEPTH, D_MODEL), 0.02),
        "ln2_b": nrm(ks[13], (DEPTH, D_MODEL), 0.02),
        "router_w": nrm(ks[14], (D_MODEL, N_EXPERTS), D_MODEL ** -0.5),
        "router_b": nrm(ks[15], (N_EXPERTS,), 0.01),
        "w_gate": nrm(ks[16], (DEPTH, N_EXPERTS, D_MODEL, D_FF), D_MODEL ** -0.5),
        "w_up": nrm(ks[17], (DEPTH, N_EXPERTS, D_MODEL, D_FF), D_MODEL ** -0.5),
        "w_down": nrm(ks[18], (DEPTH, N_EXPERTS, D_FF, D_MODEL), D_FF ** -0.5 * BETA),
    }

def reference(x, mem, conv_w_in, conv_w, mlstm_w_in, mlstm_gate_b, mlstm_norm_g, w_kv_mem, w_out,
              ln1_g, ln1_b, ln2_g, ln2_b, router_w, router_b, w_gate, w_up, w_down):
    nb, seq, d = x.shape
    for i in range(DEPTH):
        j = i // 2
        if i % 2 == 0:
            h_loc, q_mem = conv_mixer(x, conv_w_in[j], conv_w[j])
        else:
            h_loc, q_mem = mlstm_mixer(x, mlstm_w_in[j], mlstm_gate_b[j], mlstm_norm_g[j])
        h_mem = cross_attention(q_mem, mem, w_kv_mem[i])
        y = jnp.concatenate([h_loc, h_mem], axis=-1) @ w_out[i]
        x = layer_norm(ALPHA * x + y, ln1_g[i], ln1_b[i])
        m = grouped_moe(x.reshape(nb * seq, d), router_w, router_b,
                        w_gate[i], w_up[i], w_down[i]).reshape(nb, seq, d)
        x = layer_norm(ALPHA * x + m, ln2_g[i], ln2_b[i])
    return x


_drawn_inputs = setup_inputs


def setup_inputs(seed=0):
    import zlib

    import numpy as np

    out = dict(_drawn_inputs(seed))
    spreads = {}
    factors = {'mlstm_norm_g': 3.743}
    for name, (base, spread) in spreads.items():
        noise = np.random.default_rng([zlib.crc32(name.encode()), seed]).standard_normal(out[name].shape)
        drawn = base * np.exp(spread * noise) if base else spread * noise
        out[name] = __import__('jax').numpy.asarray(drawn.astype(out[name].dtype))
    for name, factor in factors.items():
        out[name] = (out[name] * factor).astype(out[name].dtype)
    return out
```

```python
import concourse.bass as bass
from concourse import mybir
from contextlib import ExitStack

F32 = mybir.dt.float32
F32R = mybir.dt.float32r
BF16 = mybir.dt.bfloat16
I32 = mybir.dt.int32
U32 = mybir.dt.uint32
ALU = mybir.AluOpType
ACT = mybir.ActivationFunctionType
AX = mybir.AxisListType

P = 128
D_MODEL = 1024
SEQ = 512
DEPTH = 2
MIX_W = 768
XATT_HEADS = 4
XATT_DH = 64
XATT_W = XATT_HEADS * XATT_DH
MEM_LEN = 256
ML_HEADS = 6
ML_DH = MIX_W // ML_HEADS
CHUNK = 128
N_CHUNKS = SEQ // CHUNK
N_EXPERTS = 32
N_GROUPS = 8
PER_GROUP = N_EXPERTS // N_GROUPS
D_FF = 512
ALPHA = (2.0 * DEPTH) ** 0.25
LN_EPS = 1e-5

TT = SEQ // P
KT = D_MODEL // P
MT = MEM_LEN // P
BLK = 64
RING = 3
W_MAT = 4096
W_EXP = 3 * W_MAT
BIG = 1e30


class Chain:

    def __init__(self, sem):
        self.sem, self.n, self.turn, self.per = sem, 0, None, 0

    def bind(self, eng):
        self.eng = eng

    def then(self, ins):
        ins.then_inc(self.sem, 1)
        self.n += 1
        at = self.n if self.turn is None else self.n + self.turn * self.per
        self.eng.wait_ge(self.sem, at)

    def loop(self, turn, per):
        self.turn, self.per, self.start = turn, per, self.n

    def end_loop(self, turns):
        assert self.n - self.start == self.per, (self.n - self.start, self.per)
        self.n += (turns - 1) * self.per
        self.turn = None


def build_trunk(nc, x, mem, conv_w_in, conv_w, mlstm_w_in, mlstm_gate_b, mlstm_norm_g, w_kv_mem, w_out,
                ln1_g, ln1_b, ln2_g, ln2_b, router_w, router_b, w_gate, w_up, w_down, out, stop=99):
    ctx = ExitStack()
    with ctx:
        phase_sems = []

        def sb(name, shape, dt=F32, at=ctx):
            return at.enter_context(nc.sbuf_tensor(name, shape, dt))

        def sem(name, at=ctx):
            if at is ctx:
                return ctx.enter_context(nc.semaphore(name))
            handle = nc.alloc_semaphore(name=name)
            phase_sems.append(handle)
            return handle

        def end_phase():
            nc.clear_and_free_semaphores(list(phase_sems))
            phase_sems.clear()
            nc.all_engine_barrier()

        ring_at = -(-nc.sbuf_base // 32) * 32
        ring = sb("ring", [P, RING * W_EXP])
        x_sb = sb("x_sb", [P, TT, D_MODEL])
        xT_at = -(-nc.sbuf_base // 32) * 32
        xT = sb("xT", [P, KT, SEQ])
        ident = sb("ident", [P, P])
        future_big = sb("future_big", [P, P])
        before = sb("before", [P, P], BF16)
        ones_bf = sb("ones_bf", [P, P], BF16)
        row_of_block = sb("row_of_block", [P, BLK])
        expert_base = sb("expert_base", [P, N_EXPERTS])
        down_from_32 = sb("down_from_32", [P, N_EXPERTS])
        tok_code = sb("tok_code", [P, TT, 2], BF16)
        half_of_row = sb("half_of_row", [P, 1])
        both_halves = sb("both_halves", [P, 2, P])
        stats, mv = sb("stats", [P, TT, 2, 6]), sb("mv", [P, TT, 4])
        eps_col = sb("eps_col", [P, 1])
        router_sb = sb("router_sb", [P, KT, N_EXPERTS])
        router_bias = sb("router_bias", [P, N_EXPERTS])
        conv_taps = sb("conv_taps", [P, 3, MIX_W // P])
        norm_g_sb = sb("norm_g_sb", [P, ML_HEADS])
        gate_bias = sb("gate_bias", [ML_HEADS, 2])
        kmT = sb("kmT", [P, 2, MEM_LEN])
        vm = sb("vm", [P, MT, XATT_W])
        slots = sb("slots", [P, TT, 2], U32)
        gates = sb("gates", [P, TT, 2])
        pos_or_none = sb("pos_or_none", [P, TT, N_EXPERTS])
        block_rows = sb("block_rows", [P, N_EXPERTS], U32)
        gate_of_expert = sb("gate_of_expert", [P, TT, N_EXPERTS])
        most_rows = sb("most_rows", [1, 1], I32)
        bank = [ctx.enter_context(nc.psum_tensor(f"bank{i}", [P, 512], F32)) for i in range(8)]

        R0, R1, R2 = (ring[:, i * W_EXP:(i + 1) * W_EXP] for i in range(RING))
        w_out_sb = R2[:, 0:8192].rearrange("p (k n) -> p k n", k=KT)
        headsT = R2[:, 8192:12288].rearrange("p (k s) -> p k s", k=KT)

        x1_dram = [nc.dram_tensor(f"x1_rows_{l}", [2 * SEQ, D_MODEL // 2], F32, kind="Internal").ap()
                   for l in range(DEPTH)]
        y_dram = [nc.dram_tensor(f"expert_rows_{l}", [N_EXPERTS * BLK, D_MODEL], F32, kind="Internal").ap()
                  for l in range(DEPTH)]

        dve_chain, act_chain, pool_chain = (Chain(sem(n)) for n in ("dve_chain", "act_chain", "pool_chain"))
        const_ready = sem("const_ready")
        in_x, in_mem, in_small = sem("in_x"), sem("in_mem"), sem("in_small")
        in_w_out = [sem(f"in_w_out{l}") for l in range(DEPTH)]
        in_slab = [sem(f"in_slab{i}") for i in range(3)]
        in_kv, in_qm = [sem(f"in_kv{l}") for l in range(DEPTH)], sem("in_qm")
        slab_turns = [0, 0, 0]
        in_gu = [[sem(f"in_gu{l}_{r}") for r in range(RING)] for l in range(DEPTH)]
        in_dn = [[sem(f"in_dn{l}_{r}") for r in range(RING)] for l in range(DEPTH)]

        def expert_views(r):
            part = ring[:, r * W_EXP:(r + 1) * W_EXP]
            gu = part[:, 0:2 * W_MAT].rearrange("p (m h c f) -> p m h c f", m=2, h=2, c=4)
            dn = part[:, 2 * W_MAT:].rearrange("p (f c d) -> p f c d", f=2, c=2)
            return gu, dn

        def load_gate_up(eng, l, e, r, done):
            part = ring[:, r * W_EXP:r * W_EXP + 2 * W_MAT].rearrange("p (m h x) -> p m h x", m=2, h=2)
            for m, w in ((0, w_gate), (1, w_up)):
                src = w[l, bass.ds(e, 1)].rearrange("o (h p c) f -> p (o h) (c f)", h=2, p=P)
                eng.dma_start(part[:, m], src).then_inc(done, 16)

        def load_down(eng, l, e, r, done):
            part = ring[:, r * W_EXP + 2 * W_MAT:(r + 1) * W_EXP].rearrange("p (f x) -> p f x", f=2)
            src = w_down[l, bass.ds(e, 1)].rearrange("o (f p c) d -> p (o f) (c d)", f=2, p=P)
            eng.dma_start(part, src).then_inc(done, 16)


        def halves_at(name, shape, hi_at, lo_at):
            return [nc.alloc_sbuf_tensor_at(f"{name}_{part}", shape, F32R, offset=at)
                    for part, at in (("hi", hi_at), ("lo", lo_at))]

        class Attention:

            def __init__(self, tag, at, qmT, kT, v, probs, probsT, vec):
                self.qmT, self.kT, self.v, self.probs, self.probsT = qmT, kT, v, probs, probsT
                self.top, self.total, self.inv = vec
                self.scored, self.maxed, self.exped, self.normed, self.turned, self.copied, self.valued, self.out = (
                    sem(f"att_{n}_{tag}", at) for n in ("scored", "maxed", "exped", "normed", "turned", "copied",
                                                        "valued", "out"))

            def pe(self, pe, step, h):
                rows = slice(64 * (h % 2), 64 * (h % 2) + 64)
                if step == "S":
                    if h:
                        pe.wait_ge(self.exped, h)
                    for t in range(TT):
                        last = nc.tensor.matmul(bank[6 + t // 2][:, (t % 2) * 256:(t % 2) * 256 + 256],
                                                self.qmT[rows, h // 2, t * P:(t + 1) * P], self.kT[rows, h // 2, :],
                                                start=True, stop=True)
                    last.then_inc(self.scored, 1)
                elif step == "T":
                    pe.wait_ge(self.normed, h + 1)
                    if h:
                        pe.wait_ge(self.copied, 2 * h)
                    for m in range(MT):
                        for t in range(TT):
                            last = nc.tensor.transpose(bank[m][:, t * P:(t + 1) * P],
                                                       self.probs[:, t, m * P:(m + 1) * P], ident[:, :])
                    last.then_inc(self.turned, 1)
                else:
                    pe.wait_ge(self.copied, 2 * h + 2)
                    if h:
                        pe.wait_ge(self.out, h)
                    for m in range(MT):
                        last = nc.tensor.matmul(bank[5][rows, :], self.v[:, m, 64 * h:64 * h + 64], self.probsT[:, m, :],
                                                start=(m == 0), stop=(m == MT - 1))
                    last.then_inc(self.valued, 1)

            def dve(self, dve, step, h):
                if step == "S":
                    dve.wait_ge(self.scored, h + 1)
                    if h:
                        dve.wait_ge(self.exped, h)
                    for b in range(2):
                        last = nc.vector.tensor_reduce(self.top[:, 2 * b:2 * b + 2],
                                                       bank[6 + b][:, :].rearrange("p (t m) -> p t m", t=2),
                                                       AX.X, ALU.max)
                    dve_chain.then(last)
                    nc.vector.tensor_scalar(self.top[:, 4:8], self.top[:, 0:4], -XATT_DH ** -0.5, None,
                                            ALU.mult).then_inc(self.maxed, 1)
                    dve.wait_ge(self.exped, h + 1)
                    dve_chain.then(nc.vector.reciprocal(self.inv[:, :], self.total[:, :]))
                    nc.vector.tensor_tensor(self.probs[:, :, :], self.probs[:, :, :],
                                            self.inv[:, :].unsqueeze(2).broadcast_to([P, TT, MEM_LEN]),
                                            ALU.mult).then_inc(self.normed, 1)
                elif step == "T":
                    dve.wait_ge(self.turned, h + 1)
                    if h:
                        dve.wait_ge(self.valued, h)
                    for m in range(MT):
                        nc.vector.tensor_copy(self.probsT[:, m, :], bank[m][:, :]).then_inc(self.copied, 1)
                else:
                    dve.wait_ge(self.valued, h + 1)
                    rows = slice(64 * (h % 2), 64 * (h % 2) + 64)
                    nc.vector.tensor_copy(headsT[rows, 6 + h // 2, :], bank[5][rows, :]).then_inc(self.out, 1)

            def act(self, act, step, h):
                if step != "S":
                    return
                act.wait_ge(self.maxed, h + 1)
                if h:
                    act.wait_ge(self.turned, h)
                for t in range(TT):
                    last = nc.scalar.activation(self.probs[:, t, :], bank[6 + t // 2][:, (t % 2) * 256:(t % 2) * 256 + 256],
                                                ACT.Exp, bias=self.top[:, 4 + t:5 + t], scale=XATT_DH ** -0.5,
                                                accum_out=self.total[:, t:t + 1])
                last.then_inc(self.exped, 1)

        def layer_norm(dve, t, g_sb, b_sb, var_ready, std_ready, scaled, done):
            xt, m = x_sb[:, t, :], mv[:, t, :]
            nc.vector.bn_stats(stats[:, t, 0, :], xt[:, 0:512])
            dve_chain.then(nc.vector.bn_stats(stats[:, t, 1, :], xt[:, 512:1024]))
            nc.vector.bn_aggr(m[:, 0:2], stats[:, t, :, :]).then_inc(var_ready, 1)
            dve.wait_ge(std_ready, t + 1)
            dve_chain.then(nc.vector.reciprocal(m[:, 2:3], m[:, 3:4]))
            dve_chain.then(nc.vector.tensor_scalar(xt, xt, m[:, 0:1], m[:, 2:3], ALU.subtract, ALU.mult))
            ins = nc.vector.tensor_tensor(xt, xt, g_sb[:, :], ALU.mult)
            if t < TT - 1:
                ins.then_inc(scaled, 1)
            else:
                dve_chain.then(ins)
                dve.wait_ge(done, t)
                nc.vector.tensor_tensor(xt, xt, b_sb[:, :], ALU.add).then_inc(done, 1)

        def add_biases(pool, b_sb, in_ln, scaled, done):
            pool.wait_ge(in_ln, 32)
            for t in range(TT - 1):
                pool.wait_ge(scaled, t + 1)
                nc.gpsimd.tensor_tensor(x_sb[:, t, :], x_sb[:, t, :], b_sb[:, :], ALU.add).then_inc(done, 1)

        def std_of_tile(act, t, var_ready, std_ready):
            act.wait_ge(var_ready, t + 1)
            nc.scalar.activation(mv[:, t, 3:4], mv[:, t, 1:2], ACT.Sqrt, bias=eps_col[:, :]).then_inc(std_ready, 1)


        def conv_phase():
            ph = ExitStack()
            ph.callback(end_phase)
            with ph:
                s = lambda n: sem(n, ph)
                slab = [R0[:, i * 3072:(i + 1) * 3072].rearrange("p (k j n) -> p k j n", k=KT, j=3) for i in range(2)]
                w_half = [halves_at(f"w_half{i}", [P, KT, P], ring_at + 4 * (6144 + 2048 * i), ring_at + 4 * (7168 + 2048 * i))
                          for i in range(3)]
                x_half = halves_at("x_half", [P, KT, SEQ], xT_at, ring_at + 4 * W_EXP)
                wkv = [R1[:, i * 4096:(i + 1) * 4096].rearrange("p (k n) -> p k n", k=KT) for i in range(2)]
                mem_sb = R1[:, 8192:10240].rearrange("p (t d) -> p t d", t=MT)
                wqm = R1[:, 8192:10240].rearrange("p (k n) -> p k n", k=KT)
                memT = R1[:, 10240:12288].rearrange("p (k m) -> p k m", k=KT)
                probs = R1[:, 10240:11264].rearrange("p (t m) -> p t m", t=TT)
                probsT = R1[:, 11264:12288].rearrange("p (m t) -> p m t", m=MT)
                kmT0 = sb("kmT0", [P, 2, MEM_LEN], at=ph)
                vm0 = sb("vm0", [P, MT, XATT_W], at=ph)
                qmT = sb("qmT0", [P, 2, SEQ], at=ph)
                cgate = sb("cgate", [P, 2, SEQ], at=ph)
                u = sb("u", [P, 2, SEQ + 2], at=ph)
                cv = sb("cv", [P, 2, SEQ], at=ph)
                vec = (sb("att_top0", [P, 8], at=ph), sb("att_sum0", [P, 4], at=ph), sb("att_inv0", [P, 4], at=ph))
                turned, copied, x_ready = s("p0_turned"), s("p0_copied"), s("p0_x_ready")
                w_hi_ready, w_lo_ready = s("p0_w_hi"), s("p0_w_lo")
                projected, by_act, by_dve = s("p0_projected"), s("p0_by_act"), s("p0_by_dve")
                att = Attention("a", ph, qmT, kmT0, vm0, probs, probsT, vec)

                script = [("tm", g) for g in range(4)] + [("km", 0, 0), ("km", 0, 1), ("vm", 0, 0), ("vm", 0, 1)]
                script += [("tx", k) for k in range(KT)]
                conv = lambda f: [("cg", f), ("xin", f), ("bg", f)]
                script += conv(0) + conv(1) + [("qm", 0), ("qm", 1)]
                script += [("km", 1, 0), ("km", 1, 1), ("vm", 1, 0), ("vm", 1, 1)]
                script += [("S", 0)] + conv(2) + [("T", 0), ("S", 1)] + conv(3) + [("V", 0), ("T", 1), ("S", 2)]
                script += conv(4) + [("V", 1), ("T", 2), ("S", 3)] + conv(5) + [("V", 2), ("T", 3), ("V", 3)]
                units = [st for st in script if st[0] in ("km", "vm", "qm", "cg", "xin", "bg")]
                on_act = ("km", "vm", "qm", "cg")
                UB = 3
                pieces = [st for st in units if st[0] in ("cg", "xin", "bg", "qm")]
                split_script = []
                for st in script:
                    if st in pieces and pieces.index(st) + 2 < len(pieces):
                        split_script.append(("W", pieces.index(st) + 2))
                    if st in (("tx", 4), ("tx", 6)):
                        split_script.append(("W", st[1] // 2 - 2))
                    split_script.append(st)

                def raw_weights(eng, i):
                    kind, f = pieces[i]
                    if kind == "qm":
                        eng.wait_ge(in_qm, 16)
                        return wqm[:, :, f * P:(f + 1) * P]
                    eng.wait_ge(in_slab[f % 2], 48 * (f // 2 + 1))
                    return slab[f % 2][:, :, ("bg", "cg", "xin").index(kind), :]

                def place_free(eng, i):
                    if i >= 3:
                        eng.wait_ge(projected, units.index(pieces[i - 3]) + 1)

                def evacuated(eng, n):
                    upto = units[:n + 1]
                    a = sum(z[0] in on_act for z in upto)
                    if units[n][0] in on_act:
                        eng.wait_ge(by_act, a)
                    else:
                        eng.wait_ge(by_dve, n + 1 - a)

                with nc.Block() as block:
                    @block.gpsimd
                    def _(pool):
                        pool_chain.bind(pool)
                        then = pool_chain.then
                        then(nc.gpsimd.memset(ident[:, :], 0.0))
                        then(nc.gpsimd.affine_select(out=ident[:, :], in_=ident[:, :], compare_op=ALU.not_equal,
                                                     fill=1.0, base=0, pattern=[[-1, P]], channel_multiplier=1))
                        then(nc.gpsimd.memset(u[:, :, 0:2], 0.0))
                        nc.gpsimd.memset(ones_bf[:, :], 1.0).then_inc(const_ready, 1)
                        then(nc.gpsimd.memset(future_big[:, :], 0.0))
                        then(nc.gpsimd.affine_select(out=future_big[:, :], in_=future_big[:, :], compare_op=ALU.is_ge,
                                                     fill=BIG, base=0, pattern=[[1, P]], channel_multiplier=-1))
                        then(nc.gpsimd.memset(before[:, :], 1.0))
                        then(nc.gpsimd.affine_select(out=before[:, :], in_=before[:, :], compare_op=ALU.is_ge,
                                                     fill=0.0, base=-1, pattern=[[1, P]], channel_multiplier=-1))
                        iota_f = lambda o, pat, base, cm: then(nc.gpsimd.iota(
                            o, pattern=pat, base=base, channel_multiplier=cm, allow_small_or_imprecise_dtypes=True))
                        iota_f(row_of_block[:, :], [[1, BLK]], 0, 0)
                        iota_f(expert_base[:, :], [[BLK, N_EXPERTS]], 0, 0)
                        iota_f(down_from_32[:, :], [[-1, N_EXPERTS]], N_EXPERTS, 0)
                        iota_f(tok_code[:, :, 0:1], [[2 * P, TT], [0, 1]], 0, 0)
                        iota_f(tok_code[:, :, 1:2], [[0, TT], [0, 1]], 0, 2)
                        then(nc.gpsimd.memset(both_halves[:, :, :], 0.0))
                        for j in range(2):
                            half = both_halves[:, j, :].rearrange("p (h r) -> p h r", h=2)
                            then(nc.gpsimd.affine_select(out=half, in_=half, compare_op=ALU.not_equal, fill=1.0,
                                                         base=-64 * j, pattern=[[0, 2], [-1, 64]], channel_multiplier=1))
                        then(nc.gpsimd.memset(eps_col[:, :], LN_EPS))
                        then(nc.gpsimd.memset(half_of_row[0:64, :], 0.0))
                        nc.gpsimd.memset(half_of_row[64:128, :], 1.0).then_inc(const_ready, 1)

                    @block.sync
                    def _(sp):
                        sp.dma_start(mem_sb, mem[0].rearrange("(t p) d -> p t d", p=P)).then_inc(in_mem, 16)
                        sp.dma_start(wkv[0], w_kv_mem[0].rearrange("(k p) n -> p k n", p=P)).then_inc(in_kv[0], 16)
                        sp.dma_start(x_sb[:, :, :], x[0].rearrange("(t p) d -> p t d", p=P)).then_inc(in_x, 16)

                        def load_slab(f):
                            if f >= 2:
                                sp.wait_ge(w_lo_ready, pieces.index(("bg", f - 2)) + 1)
                            for j in (1, 2, 0):
                                c = j * MIX_W + f * P
                                sp.dma_start(slab[f % 2][:, :, j, :], conv_w_in[0][:, c:c + P].rearrange(
                                    "(k p) n -> p k n", p=P)).then_inc(in_slab[f % 2], 16)
                        load_slab(0)
                        sp.dma_start(conv_taps[:, :, :], conv_w[0].rearrange("j (f p) -> p j f", p=P), allow_slow_non_contiguous=True).then_inc(in_small, 16)
                        sp.dma_start(router_sb[:, :, :], router_w.rearrange("(k p) n -> p k n", p=P)).then_inc(in_small, 16)
                        sp.dma_start(router_bias[:, :], router_b.unsqueeze(0).broadcast_to([P, N_EXPERTS])).then_inc(in_small, 16)
                        sp.dma_start(norm_g_sb[:, :], mlstm_norm_g[0].rearrange("(h p) -> p h", p=P), allow_slow_non_contiguous=True).then_inc(in_small, 16)
                        sp.dma_start(gate_bias[:, :], mlstm_gate_b[0].rearrange("(j h) -> h j", j=2), allow_slow_non_contiguous=True).then_inc(in_small, 16)
                        sp.wait_ge(copied, 4)
                        sp.dma_start(wqm, conv_w_in[0][:, 3 * MIX_W:].rearrange("(k p) n -> p k n", p=P)).then_inc(in_qm, 16)
                        sp.dma_start(wkv[1], w_kv_mem[1].rearrange("(k p) n -> p k n", p=P)).then_inc(in_kv[1], 16)
                        load_slab(1)
                        load_slab(2)
                        sp.dma_start(w_out_sb, w_out[0].rearrange("(k p) n -> p k n", p=P)).then_inc(in_w_out[0], 16)
                        for f in range(3, MIX_W // P):
                            load_slab(f)

                    @block.tensor
                    def _(pe):
                        pe.wait_ge(const_ready, 1)
                        groups = n = 0
                        for st in script:
                            kind = st[0]
                            if kind in ("tm", "tx"):
                                if st == ("tm", 0):
                                    pe.wait_ge(in_mem, 16)
                                if st == ("tx", 0):
                                    pe.wait_ge(in_x, 16)
                                if groups >= 6:
                                    pe.wait_ge(x_ready, groups - 5)
                                elif groups >= 2:
                                    pe.wait_ge(copied, groups - 1)
                                for j in range(4):
                                    if kind == "tm":
                                        src = mem_sb[:, j % 2, (2 * st[1] + j // 2) * P:(2 * st[1] + j // 2 + 1) * P]
                                    else:
                                        src = x_sb[:, j, st[1] * P:(st[1] + 1) * P]
                                    last = nc.tensor.transpose(bank[groups % 2][:, j * P:(j + 1) * P], src, ident[:, :])
                                last.then_inc(turned, 1)
                                groups += 1
                            elif kind in ("S", "T", "V"):
                                if st == ("S", 0):
                                    evacuated(pe, units.index(("qm", 1)))
                                att.pe(pe, kind, st[1])
                            else:
                                if n >= UB:
                                    evacuated(pe, n - UB)
                                o = bank[2 + n % UB]
                                if st == ("km", 0, 0):
                                    pe.wait_ge(in_kv[0], 16)
                                    pe.wait_ge(copied, 4)
                                if st == ("km", 1, 0):
                                    pe.wait_ge(in_kv[1], 16)
                                if st == ("cg", 0):
                                    pe.wait_ge(x_ready, KT)
                                if st in pieces:
                                    i = pieces.index(st)
                                    pe.wait_ge(w_lo_ready, i + 1)
                                for k in range(KT):
                                    fl = dict(start=(k == 0), stop=(k == KT - 1))
                                    if kind == "km":
                                        last = nc.tensor.matmul(o[:, 0:256], wkv[st[1]][:, k, st[2] * P:(st[2] + 1) * P],
                                                                memT[:, k, :], **fl)
                                    elif kind == "vm":
                                        last = nc.tensor.matmul(o[:, 0:256], memT[:, k, st[2] * P:(st[2] + 1) * P],
                                                                wkv[st[1]][:, k, 256:512], **fl)
                                    else:
                                        (w_hi, w_lo), (x_hi, x_lo) = w_half[i % 3], x_half
                                        for w, xh in ((w_hi, x_hi), (w_hi, x_lo), (w_lo, x_hi)):
                                            last = nc.tensor.matmul(o[:, :], w[:, k, :], xh[:, k, :],
                                                                    start=(k == 0 and w is w_hi and xh is x_hi),
                                                                    stop=(k == KT - 1 and w is w_lo))
                                last.then_inc(projected, 1)
                                n += 1

                    @block.scalar
                    def _(act):
                        groups = n = 0
                        for st in split_script:
                            kind = st[0]
                            if kind == "W":
                                raw = raw_weights(act, st[1])
                                place_free(act, st[1])
                                nc.scalar.copy(w_half[st[1] % 3][0][:, :, :], raw).then_inc(w_hi_ready, 1)
                            elif kind in ("tm", "tx"):
                                act.wait_ge(turned, groups + 1)
                                dst = (memT[:, 2 * st[1]:2 * st[1] + 2, :].rearrange("p k m -> p (k m)")
                                       if kind == "tm" else x_half[0][:, st[1], :])
                                nc.scalar.copy(dst, bank[groups % 2][:, :]).then_inc(copied, 1)
                                groups += 1
                            elif kind in ("S", "T", "V"):
                                att.act(act, kind, st[1])
                            else:
                                if kind in on_act:
                                    act.wait_ge(projected, n + 1)
                                    o = bank[2 + n % UB]
                                    if kind == "km":
                                        dst, o = (kmT0, kmT)[st[1]][:, st[2], :], o[:, 0:256]
                                    elif kind == "vm":
                                        dst, o = (vm0, vm)[st[1]][:, st[2], :], o[:, 0:256]
                                    elif kind == "qm":
                                        dst, o = qmT[:, st[1], :], o[:, :]
                                    else:
                                        dst, o = cgate[:, st[1] % 2, :], o[:, :]
                                        if st[1] >= 2:
                                            act.wait_ge(by_dve, 2 * st[1] - 3)
                                    nc.scalar.copy(dst, o).then_inc(by_act, 1)
                                n += 1
                        
                    @block.vector
                    def _(dve):
                        dve_chain.bind(dve)
                        then = dve_chain.then
                        n = 0
                        dve.wait_ge(const_ready, 1)
                        dve.wait_ge(in_small, 80)
                        for st in split_script:
                            kind = st[0]
                            if kind == "W":
                                raw, (hi, lo) = raw_weights(dve, st[1]), w_half[st[1] % 3]
                                dve.wait_ge(w_hi_ready, st[1] + 1)
                                nc.vector.tensor_tensor(lo[:, :, :], raw, hi[:, :, :], ALU.subtract).then_inc(w_lo_ready, 1)
                            elif kind == "tx":
                                k = st[1]
                                dve.wait_ge(copied, 5 + k)
                                nc.vector.tensor_tensor(x_half[1][:, k, :], bank[k % 2][:, :], x_half[0][:, k, :],
                                                        ALU.subtract).then_inc(x_ready, 1)
                            elif kind in ("S", "T", "V"):
                                att.dve(dve, kind, st[1])
                            elif kind in ("xin", "bg"):
                                dve.wait_ge(projected, n + 1)
                                f, o = st[1], bank[2 + n % UB]
                                ub, cb = u[:, f % 2, :], cv[:, f % 2, :]
                                if kind == "xin":
                                    evacuated(dve, n - 1)
                                    ins = nc.vector.tensor_tensor(ub[:, 2:SEQ + 2], cgate[:, f % 2, :], o[:, :], ALU.mult)
                                    ins.then_inc(by_dve, 1)
                                    dve.wait_ge(by_dve, 2 * f + 1)
                                    then(nc.vector.tensor_scalar(cb, ub[:, 0:SEQ], conv_taps[:, 0, f:f + 1], None, ALU.mult))
                                    for j in (1, 2):
                                        then(nc.vector.scalar_tensor_tensor(cb, ub[:, j:SEQ + j], conv_taps[:, j, f:f + 1],
                                                                            cb, ALU.mult, ALU.add))
                                else:
                                    nc.vector.tensor_tensor(headsT[:, f, :], cb, o[:, :], ALU.mult).then_inc(by_dve, 1)
                                    dve.wait_ge(by_dve, 2 * f + 2)
                            if kind in [z[0] for z in units]:
                                n += 1


        def out_and_route_phase(l):
            ph = ExitStack()
            ph.callback(end_phase)
            with ph:
                s = lambda n: sem(f"{n}_{l}", ph)
                ln_g, ln_b = sb(f"ln1_g_{l}", [P, D_MODEL], at=ph), sb(f"ln1_b_{l}", [P, D_MODEL], at=ph)
                per_tile = lambda n, *d: sb(f"{n}_{l}", [P, TT, *d], at=ph)
                once = lambda n, *d: sb(f"{n}_{l}", [P, *d], at=ph)
                score, one = per_tile("score", N_EXPERTS), per_tile("one", 2, N_EXPERTS)
                slot_f = per_tile("slot_f", 2)
                sel, work, near = (once(n, 2, N_EXPERTS) for n in ("sel", "work", "near"))
                gated, both = once("gated", 2, 2, N_EXPERTS), once("both", 2, 2, N_EXPERTS)
                hi1, lo1, hi2, lo2, gsum, gwork = (once(n, 2, N_GROUPS) for n in ("hi1", "lo1", "hi2", "lo2", "gsum", "gwork"))
                top, total, raw_gates, most = once("top", 2, 1), once("total", 2, 1), once("raw_gates", 2, 2), once("most", 1)
                taken = sb(f"taken_{l}", [P, TT, N_EXPERTS], BF16, at=ph)
                idx_f = sb(f"idx_f_{l}", [P, N_EXPERTS // 2], at=ph)
                onehot = sb(f"onehot_{l}", [P, 2, N_EXPERTS, BLK], BF16, at=ph)
                in_ln, out_done, summed, normed = s("p1_in_ln"), s("p1_out"), s("p1_sum"), s("p1_normed")
                turned, copied, routed, scored = s("p1_turned"), s("p1_copied"), s("p1_routed"), s("p1_scored")
                chosen, counted, marked, coded, code_read, spread_out, stored = (
                    s("p1_" + n) for n in ("chosen", "counted", "marked", "coded", "code_read", "spread_out", "stored"))
                var_ready, std_ready, scaled = s("p1_var"), s("p1_std"), s("p1_scaled")

                script = [("O", 0), ("O", 1), ("O", 2), ("O", 3), ("T", 0), ("O", 4), ("R", 0), ("O", 5), ("T", 1),
                          ("O", 6), ("R", 1), ("O", 7), ("T", 2), ("R", 2), ("P", 0), ("T", 3), ("R", 3), ("C", 0),
                          ("C", 1), ("P", 1), ("C", 2), ("C", 3)]
                POS_BANK, CODE_BANK = (bank[7], bank[0]), bank[1]
                with nc.Block() as block:
                    @block.sync
                    def _(sp):
                        for row, dst in ((ln1_g, ln_g), (ln1_b, ln_b)):
                            sp.dma_start(dst[:, :], row[l].unsqueeze(0).broadcast_to([P, D_MODEL])).then_inc(in_ln, 16)
                        for e in (0, 1):
                            load_gate_up(sp, l, e, e, in_gu[l][e])
                            load_down(sp, l, e, e, in_dn[l][e])
                        for t in range(TT):
                            sp.wait_ge(normed, t + 1)
                            sp.dma_start(x1_dram[l].rearrange("(t p h) d -> p t (h d)", t=TT, h=2)[:, t, :],
                                         x_sb[:, t, :]).then_inc(stored, 16)
                        sp.wait_ge(out_done, 2 * TT)
                        load_gate_up(sp, l, 2, 2, in_gu[l][2])
                        load_down(sp, l, 2, 2, in_dn[l][2])
                        sp.wait_ge(stored, 16 * TT)

                    @block.gpsimd
                    def _(pool):
                        add_biases(pool, ln_b, in_ln, scaled, normed)

                    @block.tensor
                    def _(pe):
                        pe.wait_ge(in_w_out[l], 16)
                        for kind, t in script:
                            if kind == "O":
                                if t >= 4:
                                    pe.wait_ge(summed, t - 3)
                                for k in range(KT):
                                    last = nc.tensor.matmul(bank[t % 4][:, :], headsT[:, k, t // 2 * P:(t // 2 + 1) * P],
                                                            w_out_sb[:, k, t % 2 * 512:(t % 2 + 1) * 512],
                                                            start=(k == 0), stop=(k == KT - 1))
                                last.then_inc(out_done, 1)
                            elif kind == "T":
                                pe.wait_ge(normed, t + 1)
                                for b in range(2):
                                    if t:
                                        pe.wait_ge(copied, 2 * t - 1 + b)
                                    for j in range(4):
                                        k = 4 * b + j
                                        last = nc.tensor.transpose(bank[4 + b][:, j * P:(j + 1) * P],
                                                                   x_sb[:, t, k * P:(k + 1) * P], ident[:, :])
                                    last.then_inc(turned, 1)
                            elif kind == "R":
                                pe.wait_ge(copied, 2 * t + 2)
                                if t:
                                    pe.wait_ge(scored, t)
                                for k in range(KT):
                                    last = nc.tensor.matmul(bank[6][:, t * 32:(t + 1) * 32], xT[:, k, t * P:(t + 1) * P],
                                                            router_sb[:, k, :], start=(k == 0), stop=(k == KT - 1))
                                last.then_inc(routed, 1)
                            elif kind == "P":
                                o = POS_BANK[t]
                                pe.wait_ge(chosen, t + 1)
                                if t:
                                    pe.wait_ge(summed, 6)
                                for j in range(2):
                                    tile = 2 * t + j
                                    for q in range(tile + 1):
                                        last = nc.tensor.matmul(o[:, 32 * j:32 * j + 32],
                                                                before[:, :] if q == tile else ones_bf[:, :],
                                                                taken[:, q, :], start=(q == 0), stop=(q == tile))
                                if t:
                                    for q in range(TT):
                                        last = nc.tensor.matmul(o[:, 64:96], ones_bf[:, :], taken[:, q, :],
                                                                start=(q == 0), stop=(q == TT - 1))
                                last.then_inc(counted, 1)
                            else:
                                pe.wait_ge(marked, t + 1)
                                if t == 0:
                                    pe.wait_ge(summed, 6)
                                for pair in range(N_EXPERTS // 2):
                                    last = nc.tensor.matmul(CODE_BANK[:, 8 * pair + 2 * t:8 * pair + 2 * t + 2],
                                                            onehot[:, t % 2, 2 * pair:2 * pair + 2, :].rearrange("p e r -> p (e r)"),
                                                            tok_code[:, t, :], start=True, stop=True)
                                last.then_inc(coded, 1)
                        pe.wait_ge(code_read, 1)
                        for j in range(2):
                            last = nc.tensor.matmul(bank[4][:, 16 * j:16 * j + 16], both_halves[:, j, :], idx_f[:, :],
                                                    start=True, stop=True)
                        last.then_inc(spread_out, 1)

                    @block.scalar
                    def _(act):
                        for kind, t in [("L", 0), ("L", 1), ("T", 0), ("R", 0), ("L", 2), ("T", 1), ("R", 1), ("T", 2),
                                        ("R", 2), ("L", 3), ("T", 3), ("R", 3)]:
                            if kind == "L":
                                std_of_tile(act, t, var_ready, std_ready)
                            elif kind == "T":
                                for b in range(2):
                                    act.wait_ge(turned, 2 * t + b + 1)
                                    nc.scalar.copy(xT[:, 4 * b:4 * b + 4, t * P:(t + 1) * P],
                                                   bank[4 + b][:, :].rearrange("p (k s) -> p k s", k=4)).then_inc(copied, 1)
                            elif kind == "R":
                                act.wait_ge(routed, t + 1)
                                nc.scalar.activation(score[:, t, :], bank[6][:, t * 32:(t + 1) * 32],
                                                     ACT.Sigmoid).then_inc(scored, 1)

                    @block.vector
                    def _(dve):
                        dve_chain.bind(dve)
                        then = dve_chain.then
                        V = nc.vector
                        order = down_from_32[:, :].unsqueeze(1).broadcast_to([P, 2, N_EXPERTS])
                        g_order = down_from_32[:, 0:N_GROUPS].unsqueeze(1).broadcast_to([P, 2, N_GROUPS])

                        def residual_and_norm(t):
                            for n in range(2):
                                dve.wait_ge(out_done, 2 * t + n + 1)
                                half = x_sb[:, t, n * 512:(n + 1) * 512]
                                V.scalar_tensor_tensor(half, half, ALPHA, bank[2 * (t % 2) + n][:, :],
                                                       ALU.mult, ALU.add).then_inc(summed, 1)
                            dve.wait_ge(summed, 2 * t + 2)
                            layer_norm(dve, t, ln_g, ln_b, var_ready, std_ready, scaled, normed)

                        def first_of_max(values, w, o, hot, width):
                            over = top[:, :, :].broadcast_to([P, 2, width])
                            then(V.tensor_reduce(top[:, :, :], values, AX.X, ALU.max))
                            then(V.tensor_tensor(w, values, over, ALU.is_equal))
                            then(V.tensor_tensor(w, w, o, ALU.mult))
                            then(V.tensor_reduce(top[:, :, :], w, AX.X, ALU.max))
                            then(V.tensor_tensor(hot, over, o, ALU.is_equal))

                        def choose(h):
                            z = slice(2 * h, 2 * h + 2)
                            dve.wait_ge(scored, 2 * h + 2)
                            then(V.tensor_tensor(sel[:, :, :], score[:, z, :],
                                                 router_bias[:, :].unsqueeze(1).broadcast_to([P, 2, N_EXPERTS]), ALU.add))
                            m = sel[:, :, :].rearrange("p t (g j) -> p t g j", j=PER_GROUP)
                            V.tensor_tensor(hi1[:, :, :], m[:, :, :, 0], m[:, :, :, 1], ALU.max)
                            V.tensor_tensor(lo1[:, :, :], m[:, :, :, 0], m[:, :, :, 1], ALU.min)
                            V.tensor_tensor(hi2[:, :, :], m[:, :, :, 2], m[:, :, :, 3], ALU.max)
                            then(V.tensor_tensor(lo2[:, :, :], m[:, :, :, 2], m[:, :, :, 3], ALU.min))
                            V.tensor_tensor(gsum[:, :, :], hi1[:, :, :], hi2[:, :, :], ALU.max)
                            V.tensor_tensor(gwork[:, :, :], hi1[:, :, :], hi2[:, :, :], ALU.min)
                            then(V.tensor_tensor(lo2[:, :, :], lo1[:, :, :], lo2[:, :, :], ALU.max))
                            then(V.tensor_tensor(gwork[:, :, :], gwork[:, :, :], lo2[:, :, :], ALU.max))
                            then(V.tensor_tensor(gsum[:, :, :], gsum[:, :, :], gwork[:, :, :], ALU.add))
                            first_of_max(gsum[:, :, :], gwork[:, :, :], g_order, hi2[:, :, :], N_GROUPS)
                            spread = lambda a: a[:, :, :].unsqueeze(3).broadcast_to([P, 2, N_GROUPS, PER_GROUP])
                            V.tensor_scalar(lo2[:, :, :], hi2[:, :, :], BIG, -BIG, ALU.mult, ALU.add)
                            then(V.tensor_tensor(m, m, spread(hi2), ALU.mult))
                            then(V.tensor_tensor(m, m, spread(lo2), ALU.add))
                            first_of_max(sel[:, :, :], work[:, :, :], order, one[:, z, 0, :], N_EXPERTS)
                            then(V.scalar_tensor_tensor(sel[:, :, :], one[:, z, 0, :], -BIG, sel[:, :, :], ALU.mult, ALU.add))
                            first_of_max(sel[:, :, :], work[:, :, :], order, one[:, z, 1, :], N_EXPERTS)
                            V.tensor_tensor(taken[:, z, :], one[:, z, 0, :], one[:, z, 1, :], ALU.add).then_inc(chosen, 1)
                            pair_of = lambda a: a.unsqueeze(2).broadcast_to([P, 2, 2, N_EXPERTS])
                            then(V.tensor_tensor(both[:, :, :, :], pair_of(score[:, z, :]), one[:, z, :, :], ALU.mult))
                            then(V.tensor_reduce(raw_gates[:, :, :], both[:, :, :, :], AX.X, ALU.add))
                            then(V.tensor_reduce(total[:, :, :], raw_gates[:, :, :], AX.X, ALU.add))
                            then(V.reciprocal(total[:, :, :], total[:, :, :]))
                            then(V.tensor_tensor(raw_gates[:, :, :], raw_gates[:, :, :], total[:, :, :].broadcast_to([P, 2, 2]),
                                                 ALU.mult))
                            then(V.tensor_tensor(gated[:, :, :, :], one[:, z, :, :],
                                                 raw_gates[:, :, :].unsqueeze(3).broadcast_to([P, 2, 2, N_EXPERTS]), ALU.mult))
                            then(V.tensor_tensor(gate_of_expert[:, z, :], gated[:, :, 0, :], gated[:, :, 1, :], ALU.add))

                        def place(h):
                            z = slice(2 * h, 2 * h + 2)
                            dve.wait_ge(counted, h + 1)
                            pos = POS_BANK[h][:, 0:64].rearrange("p (t e) -> p t e", t=2)
                            then(V.scalar_tensor_tensor(pos_or_none[:, z, :], pos, 1.0, taken[:, z, :], ALU.add, ALU.mult))
                            then(V.tensor_scalar(pos_or_none[:, z, :], pos_or_none[:, z, :], -1.0, None, ALU.add))
                            for t in (2 * h, 2 * h + 1):
                                if t >= 2:
                                    dve.wait_ge(coded, t - 1)
                                V.tensor_tensor(onehot[:, t % 2, :, :],
                                                pos_or_none[:, t, :].unsqueeze(2).broadcast_to([P, N_EXPERTS, BLK]),
                                                row_of_block[:, :].unsqueeze(1).broadcast_to([P, N_EXPERTS, BLK]),
                                                ALU.is_equal).then_inc(marked, 1)
                            pair_of = lambda a: a[:, :, :].unsqueeze(2).broadcast_to([P, 2, 2, N_EXPERTS])
                            V.scalar_tensor_tensor(sel[:, :, :], pos, float(BLK - 1),
                                                   expert_base[:, :].unsqueeze(1).broadcast_to([P, 2, N_EXPERTS]),
                                                   ALU.min, ALU.add)
                            then(V.tensor_scalar(near[:, :, :], pos, float(BLK), None, ALU.is_lt))
                            V.tensor_tensor(both[:, :, :, :], pair_of(sel), one[:, z, :, :], ALU.mult)
                            then(V.tensor_tensor(gated[:, :, :, :], pair_of(near), gated[:, :, :, :], ALU.mult))
                            V.tensor_reduce(gates[:, z, :], gated[:, :, :, :], AX.X, ALU.add)
                            then(V.tensor_reduce(slot_f[:, z, :], both[:, :, :, :], AX.X, ALU.add))
                            then(V.tensor_copy(slots[:, z, :], slot_f[:, z, :]))

                        dve.wait_ge(in_ln, 32)
                        for t in range(3):
                            residual_and_norm(t)
                        choose(0)
                        residual_and_norm(3)
                        place(0)
                        choose(1)
                        place(1)
                        then(V.tensor_reduce(most[:, :], POS_BANK[1][:, 64:96], AX.X, ALU.max))
                        then(V.tensor_copy(most_rows[0:1, 0:1], most[0:1, :]))
                        dve.wait_ge(coded, TT)
                        V.tensor_reduce(idx_f[:, :], CODE_BANK[:, 0:128].rearrange("p (e c) -> p e c", c=2 * TT),
                                        AX.X, ALU.add).then_inc(code_read, 1)
                        dve.wait_ge(spread_out, 1)
                        then(V.tensor_scalar(block_rows[:, :].rearrange("p (e j) -> p j e", j=2),
                                             bank[4][:, 0:32].rearrange("p (j e) -> p j e", j=2),
                                             half_of_row[:, :], None, ALU.add))


        def expert_phase(l):
            ph = ExitStack()
            ph.callback(end_phase)
            with ph:
                s = lambda n: sem(f"{n}_{l}", ph)
                flat = xT[:, :, :].rearrange("p k s -> p (k s)")
                part = lambda i, n: flat[:, i:i + n]
                xg = [part(512 * i, 512) for i in range(3)]
                xgT = [part(1536 + 512 * i, 512).rearrange("p (c r) -> p c r", c=4) for i in range(3)]
                silu = [part(3072 + 256 * i, 256) for i in range(3)]
                hid = [sb(f"hid{i}_{l}", [P, 256], at=ph) for i in range(3)]
                hidT = [sb(f"hidT{i}_{l}", [P, 2, P], at=ph) for i in range(3)]
                y = [sb(f"y{i}_{l}", [P, 512], at=ph) for i in range(3)]
                gathered = [s(f"p2_gathered{i}") for i in range(3)]
                stored = [s(f"p2_stored{i}") for i in range(3)]
                xturned, xcopied, gu_done, activated, hid_done = (s("p2_" + n) for n in ("xturned", "xcopied", "gu_done", "activated", "hid_done"))
                hturned, hcopied, y_done, y_copied = (s("p2_" + n) for n in ("hturned", "hcopied", "y_done", "y_copied"))
                X_BANK, H_BANK = bank[0], bank[1]
                GU_BANK, Y_BANK = bank[2:5], bank[5:8]

                with nc.Block() as block:
                    @block.sync
                    def _(sp):
                        def load(e, r):
                            sp.wait_ge(gu_done, e - 2)
                            load_gate_up(sp, l, e, r, in_gu[l][r])
                            sp.wait_ge(y_done, e - 2)
                            load_down(sp, l, e, r, in_dn[l][r])
                        with sp.Fori(0, 9) as i:
                            for r in range(3):
                                load(3 * i + (3 + r), r)
                        load(30, 0)
                        load(31, 1)

                    @block.gpsimd
                    def _(pool):
                        for e in range(N_EXPERTS):
                            if e >= 3:
                                pool.wait_ge(xturned, e - 2)
                            nc.gpsimd.indirect_dma_start(xg[e % 3], None, x1_dram[l],
                                                         bass.IndirectOffsetOnAxis(ap=block_rows[:, e:e + 1], axis=0)
                                                         ).then_inc(gathered[e % 3], 16)

                    @block.tensor
                    def _(pe):
                        def turn_rows(e, j, count):
                            pe.wait_ge(gathered[j], 16 * count)
                            if not (isinstance(e, int) and e == 0):
                                pe.wait_ge(xcopied, e)
                            for c in range(4):
                                last = nc.tensor.transpose(X_BANK[:, c * P:(c + 1) * P], xg[j][:, c::4], ident[:, :])
                            last.then_inc(xturned, 1)

                        def gate_up(e, j, count, first=False):
                            pe.wait_ge(in_gu[l][j], 32 * count)
                            pe.wait_ge(xcopied, e + 1)
                            if not first:
                                pe.wait_ge(hid_done, e - 2)
                            gu, _ = expert_views(j)
                            for h in range(2):
                                for c in range(4):
                                    for f in range(2):
                                        last = nc.tensor.matmul(GU_BANK[j][64 * f:64 * f + 64, :], xgT[j][:, c, 64 * h:64 * h + 64],
                                                                gu[:, :, h, c, 256 * f:256 * f + 256],
                                                                start=(h == 0 and c == 0), stop=(h == 1 and c == 3))
                            last.then_inc(gu_done, 1)

                        def turn_hidden(e, j):
                            pe.wait_ge(hid_done, e + 1)
                            if not (isinstance(e, int) and e == 0):
                                pe.wait_ge(hcopied, e)
                            for c in range(2):
                                last = nc.tensor.transpose(H_BANK[:, c * P:(c + 1) * P], hid[j][:, c::2], ident[:, :])
                            last.then_inc(hturned, 1)

                        def down(e, j, count, first=False):
                            pe.wait_ge(in_dn[l][j], 16 * count)
                            pe.wait_ge(hcopied, e + 1)
                            if not first:
                                pe.wait_ge(y_copied, e - 1)
                            _, dn = expert_views(j)
                            for f in range(2):
                                for c in range(2):
                                    for n in range(2):
                                        last = nc.tensor.matmul(Y_BANK[j][64 * n:64 * n + 64, :], hidT[j][:, c, 64 * f:64 * f + 64],
                                                                dn[:, f, c, 512 * n:512 * n + 512],
                                                                start=(f == 0 and c == 0), stop=(f == 1 and c == 1))
                            last.then_inc(y_done, 1)

                        turn_rows(0, 0, 1)
                        for e in range(3):
                            gate_up(e, e, 1, first=True)
                            turn_rows(e + 1, (e + 1) % 3, (e + 1) // 3 + 1)
                            if e:
                                down(e - 1, e - 1, 1, first=True)
                            turn_hidden(e, e)
                        with pe.Fori(0, 9) as i:
                            for j in range(3):
                                e = 3 * i + (3 + j)
                                gate_up(e, j, i + 2)
                                turn_rows(e + 1, (j + 1) % 3, i + (2 if j < 2 else 3))
                                down(e - 1, (j + 2) % 3, i + (2 if j else 1))
                                turn_hidden(e, j)
                        gate_up(30, 0, 11)
                        turn_rows(31, 1, 11)
                        down(29, 2, 10)
                        turn_hidden(30, 0)
                        gate_up(31, 1, 11)
                        down(30, 0, 11)
                        turn_hidden(31, 1)
                        down(31, 1, 11)

                    @block.scalar
                    def _(act):
                        def activate(e, j, first=False):
                            act.wait_ge(gu_done, e + 1)
                            if not first:
                                act.wait_ge(hid_done, e - 2)
                            nc.scalar.activation(silu[j], GU_BANK[j][:, 0:256], ACT.Silu).then_inc(activated, 1)

                        def put_out(e, j, count, first=False):
                            act.wait_ge(y_done, e + 1)
                            if not first:
                                act.wait_ge(stored[j], 32 * (count - 1))
                            nc.scalar.copy(y[j][:, :], Y_BANK[j][:, :]).then_inc(y_copied, 1)
                            act.wait_ge(y_copied, e + 1)
                            for n in range(2):
                                act.dma_start(y_dram[l][bass.ds(e * BLK, BLK), 512 * n:512 * n + 512],
                                              y[j][64 * n:64 * n + 64, :]).then_inc(stored[j], 16)

                        for e in range(3):
                            activate(e, e, first=True)
                            if e:
                                put_out(e - 1, e - 1, 1, first=True)
                        activate(3, 0)
                        put_out(2, 2, 1, first=True)
                        with act.Fori(0, 9) as i:
                            for j in range(3):
                                activate(3 * i + (4 + j), (1 + j) % 3)
                                put_out(3 * i + (3 + j), j, i + 2)
                        activate(31, 1)
                        put_out(30, 0, 11)
                        put_out(31, 1, 11)
                        act.wait_ge(stored[0], 32 * 11)
                        act.wait_ge(stored[1], 32 * 11)
                        act.wait_ge(stored[2], 32 * 10)

                    @block.vector
                    def _(dve):
                        def rows_in(e, j, first=False):
                            dve.wait_ge(xturned, e + 1)
                            if not first:
                                dve.wait_ge(gu_done, e - 2)
                            nc.vector.tensor_copy(xgT[j].rearrange("p c r -> p (c r)"), X_BANK[:, :]).then_inc(xcopied, 1)

                        def hidden(e, j, first=False):
                            dve.wait_ge(activated, e + 1)
                            if not first:
                                dve.wait_ge(hturned, e - 2)
                            nc.vector.tensor_tensor(hid[j][:, :], silu[j], GU_BANK[j][:, 256:512], ALU.mult).then_inc(hid_done, 1)
                            dve.wait_ge(hturned, e + 1)
                            if not first:
                                dve.wait_ge(y_done, e - 2)
                            nc.vector.tensor_copy(hidT[j][:, :, :].rearrange("p c r -> p (c r)"),
                                                  H_BANK[:, 0:256]).then_inc(hcopied, 1)

                        rows_in(0, 0, first=True)
                        for e in range(3):
                            rows_in(e + 1, (e + 1) % 3, first=(e < 2))
                            hidden(e, e, first=True)
                        with dve.Fori(0, 9) as i:
                            for j in range(3):
                                e = 3 * i + (3 + j)
                                rows_in(e + 1, (j + 1) % 3)
                                hidden(e, j)
                        rows_in(31, 1)
                        hidden(30, 0)
                        hidden(31, 1)


        def later_blocks_phase(l):
            ph = ExitStack()
            ph.callback(end_phase)
            with ph:
                s = lambda n: sem(f"p6_{n}_{l}", ph)
                take = lambda o, n: R0[:, o:o + n]
                later_rows = take(0, BLK)
                mark = take(64, 128).bitcast(BF16).rearrange("p (t r) -> p t r", t=TT)
                gated = take(192, 256).rearrange("p (t r) -> p t r", t=TT)
                gated2 = take(448, 512).rearrange("p (t h r) -> p t h r", t=TT, h=2)
                gatedT = take(960, 512).rearrange("p (t k) -> p t k", t=TT)
                code, idx, no_rows, rows_idx = (take(1472 + i, 1).bitcast(U32) if i else take(1472, 1) for i in range(4))
                xg, xgT = take(1536, 512), take(2048, 512).rearrange("p (c r) -> p c r", c=4)
                silu, hid = take(2560, 256), take(2816, 256)
                hidT, y = take(3072, 256).rearrange("p (c r) -> p c r", c=2), take(3328, 512)
                moved, marked, coded, code_read, indexed, gathered = (
                    s(n) for n in ("moved", "marked", "coded", "code_read", "indexed", "gathered"))
                gated_ready, xturned, xcopied, gu_done, activated, hid_done = (
                    s(n) for n in ("gated", "xturned", "xcopied", "gu_done", "activated", "hid_done"))
                hturned, hcopied, y_done, y_copied, gturned, gcopied = (
                    s(n) for n in ("hturned", "hcopied", "y_done", "y_copied", "gturned", "gcopied"))
                combined, added, in_gu1, in_dn1, gated_half, code_summed = (
                    s(n) for n in ("combined", "added", "in_gu", "in_dn", "gated_half", "code_summed"))

                def turns(eng, step, begin=None):
                    top = eng.value_load(most_rows[0:1, 0:1], min_val=0, max_val=SEQ)
                    with eng.If(top > BLK):
                        with eng.Fori(1, SEQ // BLK) as b:
                            with eng.If(top > b * BLK):
                                if begin:
                                    begin(b)
                                with eng.Fori(0, N_EXPERTS) as e:
                                    step(e, (b - 1) * N_EXPERTS + e, b)
                                eng.nop()
                            with eng.Else():
                                eng.nop()
                        eng.nop()
                    with eng.Else():
                        eng.nop()

                with nc.Block() as block:
                    @block.sync
                    def _(sp):
                        def step(e, n, b):
                            sp.wait_ge(y_done, n + 1)
                            load_gate_up(sp, l, e, 1, in_gu1)
                            load_down(sp, l, e, 1, in_dn1)
                        turns(sp, step)

                    @block.gpsimd
                    def _(pool):
                        def step(e, n, b):
                            pool.wait_ge(xturned, n + 1)
                            pool.wait_ge(code_read, n + 1)
                            nc.gpsimd.tensor_tensor(rows_idx, idx, no_rows, ALU.add).then_inc(indexed, 1)
                            pool.drain()
                            nc.gpsimd.indirect_dma_start(xg, None, x1_dram[l],
                                                         bass.IndirectOffsetOnAxis(ap=rows_idx, axis=0)).then_inc(gathered, 16)
                        turns(pool, step)

                    @block.tensor
                    def _(pe):
                        def step(e, n, b):
                            pe.wait_ge(marked, n + 1)
                            for h in range(2):
                                for t in range(TT):
                                    last = nc.tensor.matmul(bank[h][64 * h:64 * h + 64, 0:2], mark[:, t, :], tok_code[:, t, :],
                                                            start=(t == 0), stop=(t == TT - 1))
                            last.then_inc(coded, 1)
                            pe.wait_ge(gated_ready, n + 1)
                            for t in range(TT):
                                last = nc.tensor.transpose(bank[5][:, t * P:(t + 1) * P],
                                                           gated2[:, t, :, :].rearrange("p h r -> p (h r)"), ident[:, :])
                            last.then_inc(gturned, 1)
                            pe.wait_ge(gathered, 16 * (n + 1))
                            pe.wait_ge(code_read, n + 1)
                            for c in range(4):
                                last = nc.tensor.transpose(bank[1][:, c * P:(c + 1) * P], xg[:, c::4], ident[:, :])
                            last.then_inc(xturned, 1)
                            pe.wait_ge(xcopied, n + 1)
                            pe.wait_ge(in_gu1, 32 * (n + 1))
                            gu, dn = expert_views(1)
                            for h in range(2):
                                for c in range(4):
                                    for f in range(2):
                                        last = nc.tensor.matmul(bank[2][64 * f:64 * f + 64, :], xgT[:, c, 64 * h:64 * h + 64],
                                                                gu[:, :, h, c, 256 * f:256 * f + 256],
                                                                start=(h == 0 and c == 0), stop=(h == 1 and c == 3))
                            last.then_inc(gu_done, 1)
                            pe.wait_ge(hid_done, n + 1)
                            for c in range(2):
                                last = nc.tensor.transpose(bank[3][:, c * P:(c + 1) * P], hid[:, c::2], ident[:, :])
                            last.then_inc(hturned, 1)
                            pe.wait_ge(hcopied, n + 1)
                            pe.wait_ge(in_dn1, 16 * (n + 1))
                            for f in range(2):
                                for c in range(2):
                                    for m in range(2):
                                        last = nc.tensor.matmul(bank[4][64 * m:64 * m + 64, :], hidT[:, c, 64 * f:64 * f + 64],
                                                                dn[:, f, c, 512 * m:512 * m + 512],
                                                                start=(f == 0 and c == 0), stop=(f == 1 and c == 1))
                            last.then_inc(y_done, 1)
                            pe.wait_ge(gcopied, n + 1)
                            pe.wait_ge(y_copied, n + 1)
                            for t in range(TT):
                                pe.wait_ge(added, 4 * n + t + 1)
                                for m in range(2):
                                    last = nc.tensor.matmul(bank[6 + m][:, :], gatedT[64 * m:64 * m + 64, t, :],
                                                            y[64 * m:64 * m + 64, :], start=True, stop=True)
                                last.then_inc(combined, 1)
                        for free in (y_done, xturned, combined):
                            pe.sem_inc(free, 1)
                        turns(pe, step)

                    @block.scalar
                    def _(act):
                        def step(e, n, b):
                            act.wait_ge(gu_done, n + 1)
                            nc.scalar.activation(silu, bank[2][:, 0:256], ACT.Silu).then_inc(activated, 1)
                        turns(act, step)

                    @block.vector
                    def _(dve):
                        dve_chain.bind(dve)
                        V = nc.vector
                        dve.sem_inc(added, 1)
                        V.memset(no_rows, 0)
                        dve_chain.then(V.tensor_copy(later_rows, row_of_block[:, :]))

                        def begin(b):
                            V.tensor_scalar(later_rows, later_rows, float(BLK), None, ALU.add).then_inc(moved, 1)

                        def step(e, n, b):
                            col = lambda a: a[:, :, bass.ds(e, 1)].broadcast_to([P, TT, BLK])
                            dve.wait_ge(moved, b)
                            dve.wait_ge(combined, 4 * n + 1)
                            V.tensor_tensor(mark, col(pos_or_none), later_rows.unsqueeze(1).broadcast_to([P, TT, BLK]),
                                            ALU.is_equal).then_inc(marked, 1)
                            dve.wait_ge(marked, n + 1)
                            V.tensor_tensor(gated, mark, col(gate_of_expert), ALU.mult).then_inc(gated_half, 1)
                            dve.wait_ge(gated_half, n + 1)
                            V.tensor_scalar(gated2[:, :, 0, :], gated, 1.0 / ALPHA, None, ALU.mult)
                            V.tensor_scalar(gated2[:, :, 1, :], gated, 1.0 / ALPHA, None, ALU.mult).then_inc(gated_ready, 1)
                            dve.wait_ge(coded, n + 1)
                            V.tensor_reduce(code[0:64, :], bank[0][0:64, 0:2], AX.X, ALU.add)
                            V.tensor_reduce(code[64:128, :], bank[1][64:128, 0:2], AX.X, ALU.add).then_inc(code_summed, 1)
                            dve.wait_ge(code_summed, n + 1)
                            V.tensor_tensor(idx, code, half_of_row[:, :], ALU.add).then_inc(code_read, 1)
                            dve.wait_ge(gturned, n + 1)
                            V.tensor_copy(gatedT.rearrange("p t k -> p (t k)"), bank[5][:, :]).then_inc(gcopied, 1)
                            dve.wait_ge(xturned, n + 2)
                            V.tensor_copy(xgT.rearrange("p c r -> p (c r)"), bank[1][:, :]).then_inc(xcopied, 1)
                            dve.wait_ge(activated, n + 1)
                            V.tensor_tensor(hid, silu, bank[2][:, 256:512], ALU.mult).then_inc(hid_done, 1)
                            dve.wait_ge(hturned, n + 1)
                            V.tensor_copy(hidT.rearrange("p c r -> p (c r)"), bank[3][:, 0:256]).then_inc(hcopied, 1)
                            dve.wait_ge(y_done, n + 2)
                            V.tensor_copy(y, bank[4][:, :]).then_inc(y_copied, 1)
                            for t in range(TT):
                                dve.wait_ge(combined, 4 * n + t + 2)
                                for m in range(2):
                                    part = x_sb[:, t, 512 * m:512 * m + 512]
                                    last = V.tensor_tensor(part, part, bank[6 + m][:, :], ALU.add)
                                last.then_inc(added, 1)
                            dve.wait_ge(added, 4 * n + 5)
                        turns(dve, step, begin)


        def combine_phase(l):
            ph = ExitStack()
            ph.callback(end_phase)
            last_layer = l == DEPTH - 1
            with ph:
                s = lambda n: sem(f"{n}_{l}", ph)
                ln_g, ln_b = sb(f"ln2_g_{l}", [P, D_MODEL], at=ph), sb(f"ln2_b_{l}", [P, D_MODEL], at=ph)
                rows = R1[:, 0:8192].rearrange("p (i d) -> p i d", i=8)
                in_ln, normed, turned, copied, stored = (s("p3_" + n) for n in ("in_ln", "normed", "turned", "copied", "stored"))
                fetched = [s(f"p3_fetched{t}") for t in range(TT)]
                var_ready, std_ready, scaled, first_gated = s("p3_var"), s("p3_std"), s("p3_scaled"), s("p3_first")
                with nc.Block() as block:
                    @block.gpsimd
                    def _(pool):
                        for t in range(TT):
                            for g in range(2):
                                nc.gpsimd.indirect_dma_start(rows[:, 2 * t + g, :], None, y_dram[l],
                                                             bass.IndirectOffsetOnAxis(ap=slots[:, t, g:g + 1], axis=0)
                                                             ).then_inc(fetched[t], 16)
                        add_biases(pool, ln_b, in_ln, scaled, normed)

                    @block.sync
                    def _(sp):
                        for row, dst in ((ln2_g, ln_g), (ln2_b, ln_b)):
                            sp.dma_start(dst[:, :], row[l].unsqueeze(0).broadcast_to([P, D_MODEL])).then_inc(in_ln, 16)
                        if last_layer:
                            for t in range(TT):
                                sp.wait_ge(normed, t + 1)
                                sp.dma_start(out[0].rearrange("(t p) d -> p t d", t=TT)[:, t, :],
                                             x_sb[:, t, :]).then_inc(stored, 16)
                            sp.wait_ge(stored, 16 * TT)

                    @block.vector
                    def _(dve):
                        dve_chain.bind(dve)
                        then = dve_chain.then
                        dve.wait_ge(in_ln, 32)
                        for t in range(TT):
                            dve.wait_ge(fetched[t], 32)
                            xt, a, b = x_sb[:, t, :], rows[:, 2 * t, :], rows[:, 2 * t + 1, :]
                            dve.wait_ge(first_gated, t + 1)
                            then(nc.vector.scalar_tensor_tensor(a, b, gates[:, t, 1:2], a, ALU.mult, ALU.add))
                            then(nc.vector.scalar_tensor_tensor(xt, xt, ALPHA, a, ALU.mult, ALU.add))
                            layer_norm(dve, t, ln_g, ln_b, var_ready, std_ready, scaled, normed)

                    if not last_layer:
                        @block.tensor
                        def _(pe):
                            for t in range(TT):
                                pe.wait_ge(normed, t + 1)
                                for b in range(2):
                                    if t:
                                        pe.wait_ge(copied, 2 * t - 1 + b)
                                    for j in range(4):
                                        k = 4 * b + j
                                        last = nc.tensor.transpose(bank[b][:, j * P:(j + 1) * P],
                                                                   x_sb[:, t, k * P:(k + 1) * P], ident[:, :])
                                    last.then_inc(turned, 1)

                    @block.scalar
                    def _(act):
                        def gate_first(t):
                            act.wait_ge(fetched[t], 32)
                            nc.scalar.mul(rows[:, 2 * t, :], rows[:, 2 * t, :], gates[:, t, 0:1]).then_inc(first_gated, 1)

                        gate_first(0)
                        for t in range(TT):
                            if t + 1 < TT:
                                gate_first(t + 1)
                            std_of_tile(act, t, var_ready, std_ready)
                            if not last_layer:
                                for b in range(2):
                                    act.wait_ge(turned, 2 * t + b + 1)
                                    nc.scalar.copy(xT[:, 4 * b:4 * b + 4, t * P:(t + 1) * P],
                                                   bank[b][:, :].rearrange("p (k s) -> p k s", k=4)).then_inc(copied, 1)


        def mlstm_phase():
            ph = ExitStack()
            ph.callback(end_phase)
            HD = ML_DH + 1
            with ph:
                s = lambda n: sem("p4_" + n, ph)
                slab = [R0[:, i * 4096:(i + 1) * 4096].rearrange("p (k n) -> p k n", k=KT) for i in range(3)]
                take = lambda o, n: R1[:, o:o + n]
                qT = take(0, 3072).rearrange("p (h s) -> p h s", h=ML_HEADS)
                kT = take(3072, 3072).rearrange("p (h s) -> p h s", h=ML_HEADS)
                v_aug = take(6144, TT * ML_HEADS * HD).rearrange("p (t h d) -> p t h d", t=TT, h=ML_HEADS)
                probs = take(9240, 1024).rearrange("p (t m) -> p t m", t=TT)
                probsT = take(10264, 1024).rearrange("p (m t) -> p m t", m=MT)
                top_row, total_row = R1[0:ML_HEADS, 11288:11800], sb("top_next", [ML_HEADS, 1 + 2 * N_CHUNKS], at=ph)
                ogate = sb("ogate", [P, TT, MIX_W], at=ph)
                qmT = sb("qmT1", [P, 2, SEQ], at=ph)
                row_sel = sb("row_sel", [ML_HEADS, ML_HEADS, P], at=ph)
                cols = sb("cols", [P, N_CHUNKS, P], at=ph)
                vec = (sb("att_top1", [P, 8], at=ph), sb("att_sum1", [P, 4], at=ph), sb("att_inv1", [P, 4], at=ph))
                row = lambda i: headsT[0:ML_HEADS, i, :]
                in_gate, log_f, b_row, t_row, decay_out = row(0), row(1), row(2), row(3), headsT[:, 5, :]
                flat = xT[:, :, :].rearrange("p k s -> p (k s)")
                cell = lambda i, n: flat[:, i * 784:i * 784 + ML_HEADS * n].rearrange("p (h d) -> p h d", h=ML_HEADS)
                ex, S, kw, qC, state = cell(0, P), cell(1, P), cell(2, P), cell(3, HD), cell(4, HD)
                hh = qmT[:, :, :].rearrange("p j s -> p (j s)")[:, 0:ML_HEADS * P].rearrange("p (h d) -> p h d", h=ML_HEADS)
                den = sb("den", [P, ML_HEADS], at=ph)
                stat6, mv6 = sb("stat6", [P, ML_HEADS, 6], at=ph), sb("mv6", [P, ML_HEADS, 2], at=ph)
                std6 = sb("std6", [P, ML_HEADS], at=ph)
                decay = sb("decay", [P, ML_HEADS, N_CHUNKS], at=ph)

                consts, in_w = s("consts"), [s(f"in_slab{i}") for i in range(3)]
                projected, by_act, by_dve = s("projected"), s("by_act"), s("by_dve")
                g_abs, g_exp, b_ready, m_ready = s("g_abs"), s("g_exp"), s("b_ready"), s("m_ready")
                rows_ready, cols_turned, cols_ready = s("rows_ready"), s("cols_turned"), s("cols_ready")
                att = Attention("b", ph, qmT, kmT, vm, probs, probsT, vec)

                G0 = 4 * MIX_W
                slabs = [(G0, 2 * ML_HEADS + XATT_W)] + [(512 * i, 512) for i in range(6)]
                feats = lambda kind, h: (kind, h)
                script = [("gates",), ("qm", 0), ("qm", 1), ("S", 0)]
                script += [("q", h) for h in range(4)] + [("T", 0), ("S", 1)] + [("q", 4), ("q", 5), ("k", 0), ("k", 1)]
                script += [("V", 0), ("T", 1), ("S", 2)] + [("k", h) for h in range(2, 6)] + [("V", 1), ("T", 2), ("S", 3)]
                script += [("v", 3, t) for t in range(TT)] + [("V", 2), ("T", 3), ("V", 3)]
                script += [("vo", 4, t) for t in range(TT)] + [("o", 5, t) for t in range(TT)]
                units = [st for st in script if st[0] in ("gates", "qm", "q", "k", "v", "vo", "o")]
                UB = 3
                on_dve = ("gates", "v")

                def slab_of(st):
                    if st[0] in ("gates", "qm"):
                        return 0
                    if st[0] in ("q", "k"):
                        return 1 + (st[1] + (6 if st[0] == "k" else 0)) // 4
                    return 1 + st[1]
                last_of_slab = {slab_of(st): n for n, st in enumerate(units)}

                def evacuated(eng, n):
                    kinds = [z[0] for z in units[:n + 1]]
                    if kinds[n] in on_dve:
                        eng.wait_ge(by_dve, sum(z in on_dve for z in kinds))
                    else:
                        eng.wait_ge(by_act, sum(z not in on_dve for z in kinds))

                with nc.Block() as block:
                    @block.gpsimd
                    def _(pool):
                        pool_chain.bind(pool)
                        then = pool_chain.then
                        then(nc.gpsimd.memset(row_sel[:, :, :], 0.0))
                        then(nc.gpsimd.affine_select(out=row_sel[:, :, :], in_=row_sel[:, :, :], compare_op=ALU.not_equal,
                                                     fill=1.0, base=0, pattern=[[-1, ML_HEADS], [0, P]], channel_multiplier=1))
                        then(nc.gpsimd.memset(v_aug[:, :, :, ML_DH:HD], 1.0))
                        nc.gpsimd.memset(decay_out[:, :], 0.0).then_inc(consts, 1)

                    @block.sync
                    def _(sp):
                        for i, (c, w) in enumerate(slabs):
                            if i >= 3:
                                sp.wait_ge(projected, last_of_slab[i - 3] + 1)
                            sp.dma_start(slab[i % 3][:, :, 0:w], mlstm_w_in[0][:, c:c + w].rearrange("(k p) n -> p k n", p=P)
                                         ).then_inc(in_w[i % 3], 16)
                        sp.dma_start(w_out_sb, w_out[1].rearrange("(k p) n -> p k n", p=P)).then_inc(in_w_out[1], 16)

                    @block.tensor
                    def _(pe):
                        seen = set()
                        n = 0
                        for st in script:
                            kind = st[0]
                            if kind in ("S", "T", "V"):
                                if st == ("S", 0):
                                    evacuated(pe, 2)
                                att.pe(pe, kind, st[1])
                                continue
                            i = slab_of(st)
                            if i not in seen:
                                seen.add(i)
                                pe.wait_ge(in_w[i % 3], 16 * (i // 3 + 1))
                            if n >= UB:
                                evacuated(pe, n - UB)
                            o, w = bank[2 + n % UB], slab[i % 3]
                            for k in range(KT):
                                fl = dict(start=(k == 0), stop=(k == KT - 1))
                                if kind == "gates":
                                    for j in range(2):
                                        last = nc.tensor.matmul(bank[2 + 3 * j][0:ML_HEADS, :], w[:, k, j * ML_HEADS:(j + 1) * ML_HEADS],
                                                                xT[:, k, :], **fl)
                                elif kind == "qm":
                                    c = 2 * ML_HEADS + st[1] * P
                                    last = nc.tensor.matmul(o[:, :], w[:, k, c:c + P], xT[:, k, :], **fl)
                                elif kind in ("q", "k"):
                                    c = (st[1] + (6 if kind == "k" else 0)) % 4 * P
                                    last = nc.tensor.matmul(o[:, :], w[:, k, c:c + P], xT[:, k, :], **fl)
                                else:
                                    t = st[2]
                                    last = nc.tensor.matmul(o[:, :], xT[:, k, t * P:(t + 1) * P], w[:, k, :], **fl)
                            last.then_inc(projected, 1)
                            n += 1
                        pe.wait_ge(consts, 1)
                        pe.wait_ge(rows_ready, 1)
                        evacuated(pe, len(units) - 1)
                        evacuated(pe, len(units) - 2)
                        evacuated(pe, len(units) - 3)
                        for c in range(N_CHUNKS):
                            nc.tensor.transpose(bank[2][:, c * P:(c + 1) * P], decay_out[:, c * P:(c + 1) * P], ident[:, :])
                        for h in range(ML_HEADS):
                            last = nc.tensor.matmul(bank[3][:, h * N_CHUNKS:(h + 1) * N_CHUNKS], row_sel[:, h, :],
                                                    decay_out[0:ML_HEADS, P - 1::P], start=True, stop=True)
                        last.then_inc(cols_turned, 1)

                    @block.scalar
                    def _(act):
                        act_chain.bind(act)
                        then = act_chain.then
                        n = 0
                        for st in script:
                            kind = st[0]
                            if kind in ("S", "T", "V"):
                                att.act(act, kind, st[1])
                                continue
                            o = bank[2 + n % UB]
                            if kind == "gates":
                                act.wait_ge(g_abs, 1)
                                then(nc.scalar.activation(t_row, t_row, ACT.Exp, scale=-1.0))
                                nc.scalar.activation(t_row, t_row, ACT.Ln, bias=1.0).then_inc(g_exp, 1)
                            elif kind != "v":
                                act.wait_ge(projected, n + 1)
                                if kind == "qm":
                                    ins = nc.scalar.copy(qmT[:, st[1], :], o[:, :])
                                elif kind == "q":
                                    ins = nc.scalar.copy(qT[:, st[1], :], o[:, :])
                                elif kind == "k":
                                    ins = nc.scalar.mul(kT[:, st[1], :], o[:, :], ML_DH ** -0.5)
                                elif kind == "vo":
                                    nc.scalar.copy(v_aug[:, st[2], 4:6, 0:ML_DH], o[:, 0:256].rearrange("p (h d) -> p h d", h=2))
                                    ins = nc.scalar.activation(ogate[:, st[2], 0:256], o[:, 256:512], ACT.Sigmoid)
                                else:
                                    ins = nc.scalar.activation(ogate[:, st[2], 256:768], o[:, :], ACT.Sigmoid)
                                ins.then_inc(by_act, 1)
                            n += 1
                        act.wait_ge(m_ready, 1)
                        for c in range(N_CHUNKS):
                            z = slice(c * P, (c + 1) * P)
                            nc.scalar.activation(decay_out[0:ML_HEADS, z], top_row[:, z], ACT.Exp,
                                                 bias=total_row[:, c:c + 1], scale=-1.0)
                            nc.scalar.activation(decay_out[96:96 + ML_HEADS, z], in_gate[:, z], ACT.Exp,
                                                 bias=total_row[:, N_CHUNKS + 1 + c:N_CHUNKS + 2 + c])
                        nc.scalar.activation(decay_out[64:64 + ML_HEADS, :], b_row, ACT.Exp, scale=-1.0).then_inc(rows_ready, 1)

                    @block.vector
                    def _(dve):
                        dve_chain.bind(dve)
                        then = dve_chain.then
                        V = nc.vector
                        n = 0
                        dve.wait_ge(consts, 1)
                        for st in script:
                            kind = st[0]
                            if kind in ("S", "T", "V"):
                                att.dve(dve, kind, st[1])
                                continue
                            o = bank[2 + n % UB]
                            if kind == "gates":
                                dve.wait_ge(projected, 1)
                                V.tensor_scalar(in_gate, o[0:ML_HEADS, :], gate_bias[:, 0:1], None, ALU.add)
                                ins = V.tensor_scalar(log_f, bank[5][0:ML_HEADS, :], gate_bias[:, 1:2], None, ALU.add)
                                ins.then_inc(by_dve, 1)
                                dve.wait_ge(by_dve, 1)
                                V.scalar_tensor_tensor(t_row, log_f, -1.0, log_f, ALU.mult, ALU.max).then_inc(g_abs, 1)
                                dve.wait_ge(g_exp, 1)
                                then(V.scalar_tensor_tensor(log_f, log_f, 0.0, t_row, ALU.min, ALU.subtract))
                                then(V.memset(t_row, 1.0))
                                then(V.memset(total_row[:, 0:1], 0.0))
                                for c in range(N_CHUNKS):
                                    z = slice(c * P, (c + 1) * P)
                                    then(V.tensor_tensor_scan(b_row[:, z], t_row[:, z], log_f[:, z], 0.0, ALU.mult, ALU.add))
                                then(V.tensor_tensor(in_gate, in_gate, b_row, ALU.subtract))
                                for c in range(N_CHUNKS):
                                    z = slice(c * P, (c + 1) * P)
                                    at_last = slice((c + 1) * P - 1, (c + 1) * P)
                                    then(V.tensor_tensor_scan(top_row[:, z], in_gate[:, z], in_gate[:, z],
                                                              total_row[:, c:c + 1], ALU.max, ALU.max))
                                    if c < N_CHUNKS - 1:
                                        then(V.tensor_tensor(total_row[:, c + 1:c + 2], top_row[:, at_last], b_row[:, at_last],
                                                             ALU.add))
                                    then(V.tensor_scalar(total_row[:, N_CHUNKS + 1 + c:N_CHUNKS + 2 + c], top_row[:, at_last],
                                                         -1.0, None, ALU.mult))
                                then(V.tensor_copy(decay_out[32:32 + ML_HEADS, :], in_gate))
                                V.tensor_tensor(b_row, b_row, top_row, ALU.add).then_inc(m_ready, 1)
                            elif kind in on_dve:
                                dve.wait_ge(projected, n + 1)
                                V.tensor_copy(v_aug[:, st[2], 0:4, 0:ML_DH],
                                              o[:, :].rearrange("p (h d) -> p h d", h=4)).then_inc(by_dve, 1)
                            n += 1
                        dve.wait_ge(cols_turned, 1)
                        then(V.tensor_copy(cols[:, :, :].rearrange("p c x -> p (c x)"), bank[2][:, :]))
                        then(V.tensor_copy(decay[:, :, :].rearrange("p h c -> p (h c)"), bank[3][:, 0:ML_HEADS * N_CHUNKS]))

                cell_phase(ph, locals_of=dict(qT=qT, kT=kT, v_aug=v_aug, ogate=ogate, row_sel=row_sel, cols=cols, top_row=top_row,
                                              ex=ex, S=S, kw=kw, qC=qC, state=state, den=den, stat6=stat6, mv6=mv6, std6=std6,
                                              decay=decay, hh=hh))

        def cell_phase(ph, locals_of):
            d = locals_of
            qT, kT, v_aug, ogate, row_sel, cols, top_row = (d[n] for n in ("qT", "kT", "v_aug", "ogate", "row_sel", "cols", "top_row"))
            ex, S, kw, qC, state, den = (d[n] for n in ("ex", "S", "kw", "qC", "state", "den"))
            stat6, mv6, std6, decay, hh = (d[n] for n in ("stat6", "mv6", "std6", "decay", "hh"))
            HD = ML_DH + 1
            s = lambda n: sem("p5_" + n, ph)
            spread, compared, exped, weighed = s("spread"), s("compared"), s("exped"), s("weighed")
            k_turned, k_weighed, inter, intra, added = s("k_turned"), s("k_weighed"), s("inter"), s("intra"), s("added")
            updated, state_ready, var6, std_done = s("updated"), s("state_ready"), s("var6"), s("std_done")
            h_ready, h_turned, h_out, inter_read = s("h_ready"), s("h_turned"), s("h_out"), s("inter_read")
            scored = s("scored")
            pair = lambda b, w: [bank[b + i][:, 0:3 * w].rearrange("p (h d) -> p h d", h=3) for i in range(2)]
            W_COL, C_COL, EM_COL, WS_COL = 0, 32, 64, 96
            with nc.Block() as block:
                @block.tensor
                def _(pe):
                    def front(c):
                        z = slice(c * P, (c + 1) * P)
                        if c > 1:
                            pe.wait_ge(h_out, 2 * (c - 1))
                        elif c:
                            pe.wait_ge(k_weighed, c)
                        for h in range(ML_HEADS):
                            last = nc.tensor.matmul(pair(0, P)[h // 3][:, h % 3, :], row_sel[:, h, :], top_row[:, z],
                                                    start=True, stop=True)
                        last.then_inc(spread, 1)
                        if c:
                            pe.wait_ge(state_ready, c)
                        for h in range(ML_HEADS):
                            last = nc.tensor.matmul(pair(2, P)[h // 3][:, h % 3, :], kT[:, h, z], qT[:, h, z], start=True, stop=True)
                        last.then_inc(scored, 1)
                        if c < N_CHUNKS - 1:
                            pe.wait_ge(compared, c + 1)
                            for h in range(ML_HEADS):
                                last = nc.tensor.transpose(pair(0, P)[h // 3][:, h % 3, :], kT[:, h, z], ident[:, :])
                            last.then_inc(k_turned, 1)

                    def turn_out(c):
                        pe.wait_ge(h_ready, c + 1)
                        if c + 1 < N_CHUNKS - 1:
                            pe.wait_ge(k_weighed, c + 2)
                        else:
                            pe.wait_ge(compared, N_CHUNKS)
                        for h in range(ML_HEADS):
                            last = nc.tensor.transpose(pair(0, P)[h // 3][:, h % 3, :], hh[:, h, :], ident[:, :])
                        last.then_inc(h_turned, 1)

                    front(0)
                    for c in range(N_CHUNKS):
                        z = slice(c * P, (c + 1) * P)
                        if c:
                            if c > 1:
                                pe.wait_ge(inter_read, c - 1)
                            pe.wait_ge(state_ready, c)
                            for h in range(ML_HEADS):
                                last = nc.tensor.matmul(pair(6, HD)[h // 3][:, h % 3, :], qT[:, h, z], state[:, h, :],
                                                        start=True, stop=True)
                            last.then_inc(inter, 1)
                        pe.wait_ge(weighed, c + 1)
                        if c:
                            pe.wait_ge(added, c)
                        for h in range(ML_HEADS):
                            last = nc.tensor.matmul(pair(4, HD)[h // 3][:, h % 3, :], S[:, h, :], v_aug[:, c, h, :],
                                                    start=True, stop=True)
                        last.then_inc(intra, 1)
                        if c < N_CHUNKS - 1:
                            pe.wait_ge(k_weighed, c + 1)
                            for h in range(ML_HEADS):
                                last = nc.tensor.matmul(pair(2, HD)[h // 3][:, h % 3, :], kw[:, h, :], v_aug[:, c, h, :],
                                                        start=True, stop=True)
                            last.then_inc(updated, 1)
                        if c:
                            turn_out(c - 1)
                        if c < N_CHUNKS - 1:
                            front(c + 1)
                    turn_out(N_CHUNKS - 1)

                @block.scalar
                def _(act):
                    def write_out(c):
                        act.wait_ge(h_turned, c + 1)
                        for i in range(2):
                            for j in range(3):
                                h = 3 * i + j
                                last = nc.scalar.mul(headsT[:, h, c * P:(c + 1) * P], pair(0, P)[i][:, j, :], norm_g_sb[:, h:h + 1])
                            last.then_inc(h_out, 1)

                    for c in range(N_CHUNKS):
                        act.wait_ge(compared, c + 1)
                        nc.scalar.activation(ex[:, :, :], ex[:, :, :], ACT.Exp, scale=-1.0).then_inc(exped, 1)
                        if c:
                            act.wait_ge(var6, c)
                            nc.scalar.activation(std6[:, :], mv6[:, :, 1], ACT.Sqrt, bias=eps_col[:, :]).then_inc(std_done, 1)
                            write_out(c - 1)
                    act.wait_ge(var6, N_CHUNKS)
                    nc.scalar.activation(std6[:, :], mv6[:, :, 1], ACT.Sqrt, bias=eps_col[:, :]).then_inc(std_done, 1)
                    write_out(N_CHUNKS - 1)

                @block.vector
                def _(dve):
                    dve_chain.bind(dve)
                    then = dve_chain.then
                    V = nc.vector
                    three = lambda a, i: a[:, 3 * i:3 * i + 3, :]
                    col = lambda c, kind, i, w: cols[:, c, kind + 3 * i:kind + 3 * i + 3].unsqueeze(2).broadcast_to([P, 3, w])

                    def compare(c):
                        dve.wait_ge(spread, c + 1)
                        if c:
                            dve.wait_ge(weighed, c)
                        for h in range(ML_HEADS):
                            last = V.scalar_tensor_tensor(ex[:, h, :], pair(0, P)[h // 3][:, h % 3, :],
                                                          cols[:, c, C_COL + h:C_COL + h + 1], future_big[:, :],
                                                          ALU.subtract, ALU.max)
                        last.then_inc(compared, 1)

                    def weigh_keys(c):
                        dve.wait_ge(k_turned, c + 1)
                        if c:
                            dve.wait_ge(updated, c)
                        for i in range(2):
                            last = V.tensor_tensor(three(kw, i), pair(0, P)[i], col(c, WS_COL, i, P), ALU.mult)
                        last.then_inc(k_weighed, 1)

                    def weigh_scores(c):
                        dve.wait_ge(exped, c + 1)
                        dve.wait_ge(scored, c + 1)
                        if c:
                            dve.wait_ge(intra, c)
                        for i in range(2):
                            last = V.tensor_tensor(three(S, i), pair(2, P)[i], three(ex, i), ALU.mult)
                        last.then_inc(weighed, 1)

                    def sums_and_state(c):
                        if c:
                            dve.wait_ge(inter, c)
                            for i in range(2):
                                last = V.tensor_tensor(three(qC, i), pair(6, HD)[i], col(c, W_COL, i, HD), ALU.mult)
                            last.then_inc(inter_read, 1)
                            dve.wait_ge(inter_read, c)
                        dve.wait_ge(intra, c + 1)
                        for i in range(2):
                            if c:
                                last = V.tensor_tensor(three(qC, i), pair(4, HD)[i], three(qC, i), ALU.add)
                            else:
                                last = V.tensor_copy(three(qC, i), pair(4, HD)[i])
                        last.then_inc(added, 1)
                        dve.wait_ge(added, c + 1)
                        if c < N_CHUNKS - 1:
                            dve.wait_ge(updated, c + 1)
                            for h in range(ML_HEADS):
                                new = pair(2, HD)[h // 3][:, h % 3, :]
                                if c:
                                    last = V.scalar_tensor_tensor(state[:, h, :], state[:, h, :], decay[:, h, c:c + 1], new,
                                                                  ALU.mult, ALU.add)
                                else:
                                    last = V.tensor_copy(state[:, h, :], new)
                            last.then_inc(state_ready, 1)

                    def divide(c):
                        dcol = qC[:, :, ML_DH]
                        then(V.scalar_tensor_tensor(den[:, :], dcol, -1.0, dcol, ALU.mult, ALU.max))
                        then(V.tensor_tensor(den[:, :], den[:, :], cols[:, c, EM_COL:EM_COL + ML_HEADS], ALU.max))
                        then(V.reciprocal(den[:, :], den[:, :]))
                        if c:
                            dve.wait_ge(h_turned, c)
                        then(V.tensor_tensor(hh[:, :, :], qC[:, :, 0:ML_DH], den[:, :].unsqueeze(2).broadcast_to([P, ML_HEADS, ML_DH]),
                                             ALU.mult))
                        for h in range(ML_HEADS):
                            last = V.bn_stats(stat6[:, h, :], hh[:, h, :])
                        then(last)
                        for h in range(ML_HEADS):
                            last = V.bn_aggr(mv6[:, h, :], stat6[:, h, :])
                        last.then_inc(var6, 1)

                    def norm(c):
                        dve.wait_ge(std_done, c + 1)
                        then(V.reciprocal(std6[:, :], std6[:, :]))
                        for h in range(ML_HEADS):
                            last = V.tensor_scalar(hh[:, h, :], hh[:, h, :], mv6[:, h, 0:1], std6[:, h:h + 1], ALU.subtract, ALU.mult)
                        then(last)
                        V.tensor_tensor(hh[:, :, :], hh[:, :, :], ogate[:, c, :].rearrange("p (h d) -> p h d", h=ML_HEADS),
                                        ALU.mult).then_inc(h_ready, 1)

                    compare(0)
                    weigh_keys(0)
                    weigh_scores(0)
                    for c in range(N_CHUNKS):
                        sums_and_state(c)
                        if c < N_CHUNKS - 1:
                            if c:
                                norm(c - 1)
                            compare(c + 1)
                        elif c:
                            norm(c - 1)
                        divide(c)
                        if c < N_CHUNKS - 2:
                            weigh_keys(c + 1)
                        if c < N_CHUNKS - 1:
                            weigh_scores(c + 1)
                    norm(N_CHUNKS - 1)

        def dump():
            done = sem("dumped")
            with nc.Block() as block:
                @block.sync
                def _(sp):
                    sp.dma_start(out[0].rearrange("(t p) d -> p t d", t=TT), x_sb[:, :, :]).then_inc(done, 16)
                    sp.wait_ge(done, 16)
        conv_phase()
        out_and_route_phase(0)
        if stop == 1:
            return dump()
        expert_phase(0)
        later_blocks_phase(0)
        combine_phase(0)
        if stop == 3:
            return dump()
        mlstm_phase()
        out_and_route_phase(1)
        if stop == 5:
            return dump()
        expert_phase(1)
        later_blocks_phase(1)
        combine_phase(1)


_INS = ['x', 'mem', 'conv_w_in', 'conv_w', 'mlstm_w_in', 'mlstm_gate_b', 'mlstm_norm_g', 'w_kv_mem', 'w_out',
        'ln1_g', 'ln1_b', 'ln2_g', 'ln2_b', 'router_w', 'router_b', 'w_gate', 'w_up', 'w_down']


def kernel(**inputs):
    import numpy as _np
    import concourse.bacc as _bacc
    from concourse.bass_utils import run_bass_kernel_spmd as _run

    nc = _bacc.Bacc("TRN2", target_bir_lowering=False, num_devices=1)
    arrays, args = {}, []
    for name in _INS:
        a = _np.ascontiguousarray(inputs[name])
        arrays[f"in_{name}"] = a
        args.append(nc.dram_tensor(f"in_{name}", a.shape, mybir.dt.from_np(a.dtype), kind="ExternalInput").ap())
    out = nc.dram_tensor("out", (1, SEQ, D_MODEL), F32, kind="ExternalOutput").ap()
    build_trunk(nc, *args, out)
    r = _run(nc, [arrays], core_ids=[0])
    return r.results[0]["out"]
```

```python
import concourse.bass as bass
from concourse import mybir
from contextlib import ExitStack

F32 = mybir.dt.float32
F32R = mybir.dt.float32r
BF16 = mybir.dt.bfloat16
I32 = mybir.dt.int32
U32 = mybir.dt.uint32
ALU = mybir.AluOpType
ACT = mybir.ActivationFunctionType
AX = mybir.AxisListType

P = 128
D_MODEL = 1024
SEQ = 512
DEPTH = 2
MIX_W = 768
XATT_HEADS = 4
XATT_DH = 64
XATT_W = XATT_HEADS * XATT_DH
MEM_LEN = 256
ML_HEADS = 6
ML_DH = MIX_W // ML_HEADS
CHUNK = 128
N_CHUNKS = SEQ // CHUNK
N_EXPERTS = 32
N_GROUPS = 8
PER_GROUP = N_EXPERTS // N_GROUPS
D_FF = 512
ALPHA = (2.0 * DEPTH) ** 0.25
LN_EPS = 1e-5

TT = SEQ // P
KT = D_MODEL // P
MT = MEM_LEN // P
BLK = 64
RING = 3
W_MAT = 4096
W_EXP = 3 * W_MAT
BIG = 1e30


class Chain:

    def __init__(self, sem):
        self.sem, self.n = sem, 0

    def bind(self, eng):
        self.eng = eng

    def then(self, ins):
        ins.then_inc(self.sem, 1)
        self.n += 1
        self.eng.wait_ge(self.sem, self.n)


def build_trunk(nc, x, mem, conv_w_in, conv_w, mlstm_w_in, mlstm_gate_b, mlstm_norm_g, w_kv_mem, w_out,
                ln1_g, ln1_b, ln2_g, ln2_b, router_w, router_b, w_gate, w_up, w_down, out, stop=99):
    ctx = ExitStack()
    with ctx:
        phase_sems = []

        def sb(name, shape, dt=F32, at=ctx):
            return at.enter_context(nc.sbuf_tensor(name, shape, dt))

        def sem(name, at=ctx):
            if at is ctx:
                return ctx.enter_context(nc.semaphore(name))
            handle = nc.alloc_semaphore(name=name)
            phase_sems.append(handle)
            return handle

        def end_phase():
            nc.clear_and_free_semaphores(list(phase_sems))
            phase_sems.clear()
            nc.all_engine_barrier()

        ring_at = -(-nc.sbuf_base // 32) * 32
        ring = sb("ring", [P, RING * W_EXP])
        x_sb = sb("x_sb", [P, TT, D_MODEL])
        xT_at = -(-nc.sbuf_base // 32) * 32
        xT = sb("xT", [P, KT, SEQ])
        ident = sb("ident", [P, P])
        future_big = sb("future_big", [P, P])
        before = sb("before", [P, P], BF16)
        ones_bf = sb("ones_bf", [P, P], BF16)
        row_of_block = sb("row_of_block", [P, BLK])
        expert_base = sb("expert_base", [P, N_EXPERTS])
        down_from_32 = sb("down_from_32", [P, N_EXPERTS])
        tok_code = sb("tok_code", [P, TT, 2], BF16)
        half_of_row = sb("half_of_row", [P, 1])
        both_halves = sb("both_halves", [P, 2, P])
        stats, mv = sb("stats", [P, TT, 2, 6]), sb("mv", [P, TT, 4])
        eps_col = sb("eps_col", [P, 1])
        router_sb = sb("router_sb", [P, KT, N_EXPERTS])
        router_bias = sb("router_bias", [P, N_EXPERTS])
        conv_taps = sb("conv_taps", [P, 3, MIX_W // P])
        norm_g_sb = sb("norm_g_sb", [P, ML_HEADS])
        gate_bias = sb("gate_bias", [32 + ML_HEADS, 1])
        kmT = sb("kmT", [P, 2, MEM_LEN])
        vm = sb("vm", [P, MT, XATT_W])
        slots = sb("slots", [P, TT, 2], U32)
        gates = sb("gates", [P, TT, 2])
        pos_or_none = sb("pos_or_none", [P, TT, N_EXPERTS])
        block_rows = sb("block_rows", [P, N_EXPERTS], U32)
        gate_of_expert = sb("gate_of_expert", [P, TT, N_EXPERTS])
        most_rows = sb("most_rows", [1, 1], I32)
        bank = [ctx.enter_context(nc.psum_tensor(f"bank{i}", [P, 512], F32)) for i in range(8)]

        R0, R1, R2 = (ring[:, i * W_EXP:(i + 1) * W_EXP] for i in range(RING))
        w_out_sb = R2[:, 0:8192].rearrange("p (k n) -> p k n", k=KT)
        headsT = R2[:, 8192:12288].rearrange("p (k s) -> p k s", k=KT)

        x1_dram = [nc.dram_tensor(f"x1_rows_{l}", [2 * SEQ, D_MODEL // 2], F32, kind="Internal").ap()
                   for l in range(DEPTH)]
        y_dram = [nc.dram_tensor(f"expert_rows_{l}", [N_EXPERTS * BLK, D_MODEL], F32, kind="Internal").ap()
                  for l in range(DEPTH)]

        dve_chain, act_chain, pool_chain = (Chain(sem(n)) for n in ("dve_chain", "act_chain", "pool_chain"))
        const_ready = sem("const_ready")
        in_x, in_mem, in_small = sem("in_x"), sem("in_mem"), sem("in_small")
        in_w_out = [sem(f"in_w_out{l}") for l in range(DEPTH)]
        in_slab, in_w = ([sem(f"{n}{i}") for i in range(2)] for n in ("in_slab", "in_w"))
        in_kv, in_qm = [sem(f"in_kv{l}") for l in range(DEPTH)], sem("in_qm")
        in_gu = [[sem(f"in_gu{l}_{r}") for r in range(RING)] for l in range(DEPTH)]
        in_dn = [[sem(f"in_dn{l}_{r}") for r in range(RING)] for l in range(DEPTH)]

        def expert_views(r):
            part = ring[:, r * W_EXP:(r + 1) * W_EXP]
            gu = part[:, 0:2 * W_MAT].rearrange("p (m h c f) -> p m h c f", m=2, h=2, c=4)
            dn = part[:, 2 * W_MAT:].rearrange("p (f c d) -> p f c d", f=2, c=2)
            return gu, dn

        def load_gate_up(eng, l, e, r, done):
            part = ring[:, r * W_EXP:r * W_EXP + 2 * W_MAT].rearrange("p (m h x) -> p m h x", m=2, h=2)
            for m, w in ((0, w_gate), (1, w_up)):
                src = w[l, bass.ds(e, 1)].rearrange("o (h p c) f -> p (o h) (c f)", h=2, p=P)
                eng.dma_start(part[:, m], src).then_inc(done, 16)

        def load_down(eng, l, e, r, done):
            part = ring[:, r * W_EXP + 2 * W_MAT:(r + 1) * W_EXP].rearrange("p (f x) -> p f x", f=2)
            src = w_down[l, bass.ds(e, 1)].rearrange("o (f p c) d -> p (o f) (c d)", f=2, p=P)
            eng.dma_start(part, src).then_inc(done, 16)


        def halves_at(name, shape, hi_at, lo_at):
            return [nc.alloc_sbuf_tensor_at(f"{name}_{part}", shape, F32R, offset=at)
                    for part, at in (("hi", hi_at), ("lo", lo_at))]

        class Attention:

            def __init__(self, tag, at, qmT, kT, v, probs, probsT, vec):
                self.qmT, self.kT, self.v, self.probs, self.probsT = qmT, kT, v, probs, probsT
                self.top, self.total, self.inv = vec
                self.scored, self.maxed, self.exped, self.normed, self.turned, self.copied, self.valued, self.out = (
                    sem(f"att_{n}_{tag}", at) for n in ("scored", "maxed", "exped", "normed", "turned", "copied",
                                                        "valued", "out"))

            def pe(self, pe, step, h):
                rows = slice(64 * (h % 2), 64 * (h % 2) + 64)
                if step == "S":
                    if h:
                        pe.wait_ge(self.exped, h)
                    for t in range(TT):
                        last = nc.tensor.matmul(bank[6 + t // 2][:, (t % 2) * 256:(t % 2) * 256 + 256],
                                                self.qmT[rows, h // 2, t * P:(t + 1) * P], self.kT[rows, h // 2, :],
                                                start=True, stop=True)
                    last.then_inc(self.scored, 1)
                elif step == "T":
                    pe.wait_ge(self.normed, h + 1)
                    if h:
                        pe.wait_ge(self.copied, 2 * h)
                    for m in range(MT):
                        for t in range(TT):
                            last = nc.tensor.transpose(bank[m][:, t * P:(t + 1) * P],
                                                       self.probs[:, t, m * P:(m + 1) * P], ident[:, :])
                    last.then_inc(self.turned, 1)
                else:
                    pe.wait_ge(self.copied, 2 * h + 2)
                    if h:
                        pe.wait_ge(self.out, h)
                    for m in range(MT):
                        last = nc.tensor.matmul(bank[5][rows, :], self.v[:, m, 64 * h:64 * h + 64], self.probsT[:, m, :],
                                                start=(m == 0), stop=(m == MT - 1))
                    last.then_inc(self.valued, 1)

            def dve(self, dve, step, h):
                if step == "S":
                    dve.wait_ge(self.scored, h + 1)
                    if h:
                        dve.wait_ge(self.exped, h)
                    for b in range(2):
                        last = nc.vector.tensor_reduce(self.top[:, 2 * b:2 * b + 2],
                                                       bank[6 + b][:, :].rearrange("p (t m) -> p t m", t=2),
                                                       AX.X, ALU.max)
                    dve_chain.then(last)
                    nc.vector.tensor_scalar(self.top[:, 4:8], self.top[:, 0:4], -XATT_DH ** -0.5, None,
                                            ALU.mult).then_inc(self.maxed, 1)
                    dve.wait_ge(self.exped, h + 1)
                    dve_chain.then(nc.vector.reciprocal(self.inv[:, :], self.total[:, :]))
                    nc.vector.tensor_tensor(self.probs[:, :, :], self.probs[:, :, :],
                                            self.inv[:, :].unsqueeze(2).broadcast_to([P, TT, MEM_LEN]),
                                            ALU.mult).then_inc(self.normed, 1)
                elif step == "T":
                    dve.wait_ge(self.turned, h + 1)
                    if h:
                        dve.wait_ge(self.valued, h)
                    for m in range(MT):
                        nc.vector.tensor_copy(self.probsT[:, m, :], bank[m][:, :]).then_inc(self.copied, 1)
                else:
                    dve.wait_ge(self.valued, h + 1)
                    rows = slice(64 * (h % 2), 64 * (h % 2) + 64)
                    nc.vector.tensor_copy(headsT[rows, 6 + h // 2, :], bank[5][rows, :]).then_inc(self.out, 1)

            def act(self, act, step, h):
                if step != "S":
                    return
                act.wait_ge(self.maxed, h + 1)
                if h:
                    act.wait_ge(self.turned, h)
                for t in range(TT):
                    last = nc.scalar.activation(self.probs[:, t, :], bank[6 + t // 2][:, (t % 2) * 256:(t % 2) * 256 + 256],
                                                ACT.Exp, bias=self.top[:, 4 + t:5 + t], scale=XATT_DH ** -0.5,
                                                accum_out=self.total[:, t:t + 1])
                last.then_inc(self.exped, 1)

        def layer_norm(dve, t, g_sb, b_sb, var_ready, std_ready, scaled, done):
            xt, m = x_sb[:, t, :], mv[:, t, :]
            moments(t, var_ready)
            dve.wait_ge(std_ready, t + 1)
            dve_chain.then(nc.vector.reciprocal(m[:, 2:3], m[:, 3:4]))
            dve_chain.then(nc.vector.tensor_scalar(xt, xt, m[:, 0:1], m[:, 2:3], ALU.subtract, ALU.mult))
            scale_and_shift(dve, t, g_sb, b_sb, scaled, done)

        def moments(t, var_ready):
            nc.vector.bn_stats(stats[:, t, 0, :], x_sb[:, t, 0:512])
            dve_chain.then(nc.vector.bn_stats(stats[:, t, 1, :], x_sb[:, t, 512:1024]))
            nc.vector.bn_aggr(mv[:, t, 0:2], stats[:, t, :, :]).then_inc(var_ready, 1)

        def scale_and_shift(dve, t, g_sb, b_sb, scaled, done):
            xt = x_sb[:, t, :]
            ins = nc.vector.tensor_tensor(xt, xt, g_sb[:, :], ALU.mult)
            if t < TT - 1:
                ins.then_inc(scaled, 1)
            else:
                dve_chain.then(ins)
                dve.wait_ge(done, t)
                nc.vector.tensor_tensor(xt, xt, b_sb[:, :], ALU.add).then_inc(done, 1)

        def add_biases(pool, b_sb, in_ln, scaled, done):
            pool.wait_ge(in_ln, 32)
            for t in range(TT - 1):
                pool.wait_ge(scaled, t + 1)
                nc.gpsimd.tensor_tensor(x_sb[:, t, :], x_sb[:, t, :], b_sb[:, :], ALU.add).then_inc(done, 1)

        def std_of_tile(act, t, var_ready, std_ready):
            act.wait_ge(var_ready, t + 1)
            nc.scalar.activation(mv[:, t, 3:4], mv[:, t, 1:2], ACT.Sqrt, bias=eps_col[:, :]).then_inc(std_ready, 1)

        x2_half = halves_at("x2_half", [P, KT, SEQ], xT_at, ring_at + 4 * 2 * W_EXP)


        def conv_phase():
            ph = ExitStack()
            ph.callback(end_phase)
            with ph:
                s = lambda n: sem(n, ph)
                slab = [R0[:, i * 3072:(i + 1) * 3072].rearrange("p (k j n) -> p k j n", k=KT, j=3) for i in range(2)]
                w_half = [halves_at(f"w_half{i}", [P, KT, P], ring_at + 4 * (6144 + 2048 * i), ring_at + 4 * (7168 + 2048 * i))
                          for i in range(3)]
                x_half = halves_at("x_half", [P, KT, SEQ], xT_at, ring_at + 4 * W_EXP)
                wkv = [a.rearrange("p (k n) -> p k n", k=KT) for a in (R2[:, 0:4096], R1[:, 4096:8192])]
                mem_sb = R1[:, 8192:10240].rearrange("p (t d) -> p t d", t=MT)
                wqm = R1[:, 8192:10240].rearrange("p (k n) -> p k n", k=KT)
                memT = R1[:, 10240:12288].rearrange("p (k m) -> p k m", k=KT)
                probs = R1[:, 10240:11264].rearrange("p (t m) -> p t m", t=TT)
                probsT = R1[:, 11264:12288].rearrange("p (m t) -> p m t", m=MT)
                kmT0 = sb("kmT0", [P, 2, MEM_LEN], at=ph)
                vm0 = sb("vm0", [P, MT, XATT_W], at=ph)
                qmT = sb("qmT0", [P, 2, SEQ], at=ph)
                cgate = sb("cgate", [P, 2, SEQ], at=ph)
                u = sb("u", [P, 2, SEQ + 2], at=ph)
                cv = sb("cv", [P, 2, SEQ], at=ph)
                vec = (sb("att_top0", [P, 8], at=ph), sb("att_sum0", [P, 4], at=ph), sb("att_inv0", [P, 4], at=ph))
                turned, copied, x_ready = s("p0_turned"), s("p0_copied"), s("p0_x_ready")
                w_hi_ready, w_lo_ready = s("p0_w_hi"), s("p0_w_lo")
                projected, by_act, by_dve = s("p0_projected"), s("p0_by_act"), s("p0_by_dve")
                att = Attention("a", ph, qmT, kmT0, vm0, probs, probsT, vec)

                script = [("tm", g) for g in range(4)] + [("km", 0, 0), ("km", 0, 1), ("tx", 0), ("tx", 1), ("vm", 0, 0)]
                script += [("tx", k) for k in (2, 3, 4)] + [("vm", 0, 1)] + [("tx", k) for k in (5, 6, 7)]
                conv = lambda f: [("cg", f), ("xin", f), ("bg", f)]
                script += conv(0) + conv(1) + [("qm", 0), ("qm", 1)]
                script += [("km", 1, 0), ("km", 1, 1), ("vm", 1, 0), ("vm", 1, 1)]
                script += [("S", 0)] + conv(2) + [("T", 0), ("S", 1)] + conv(3) + [("V", 0), ("T", 1), ("S", 2)]
                script += conv(4) + [("V", 1), ("T", 2), ("S", 3)] + conv(5) + [("V", 2), ("T", 3), ("V", 3)]
                units = [st for st in script if st[0] in ("km", "vm", "qm", "cg", "xin", "bg")]
                on_act = ("km", "vm", "qm", "cg")
                UB = 3
                pieces = [st for st in units if st[0] in ("cg", "xin", "bg", "qm")]
                split_script = []
                for st in script:
                    if st == ("tx", 4):
                        split_script.append(("W", 0))
                    if st == pieces[0]:
                        split_script.append(("W", 1))
                    if st in pieces and pieces.index(st) + 2 < len(pieces):
                        split_script.append(("W", pieces.index(st) + 2))
                    split_script.append(st)

                def raw_weights(eng, i):
                    kind, f = pieces[i]
                    if kind == "qm":
                        eng.wait_ge(in_qm, 16)
                        return wqm[:, :, f * P:(f + 1) * P]
                    eng.wait_ge(in_slab[f % 2], 48 * (f // 2 + 1))
                    return slab[f % 2][:, :, ("bg", "cg", "xin").index(kind), :]

                def place_free(eng, i):
                    if i >= 3:
                        eng.wait_ge(projected, units.index(pieces[i - 3]) + 1)

                def evacuated(eng, n):
                    upto = units[:n + 1]
                    a = sum(z[0] in on_act for z in upto)
                    if units[n][0] in on_act:
                        eng.wait_ge(by_act, a)
                    else:
                        eng.wait_ge(by_dve, n + 1 - a)

                with nc.Block() as block:
                    @block.gpsimd
                    def _(pool):
                        pool_chain.bind(pool)
                        then = pool_chain.then
                        then(nc.gpsimd.memset(ident[:, :], 0.0))
                        then(nc.gpsimd.affine_select(out=ident[:, :], in_=ident[:, :], compare_op=ALU.not_equal,
                                                     fill=1.0, base=0, pattern=[[-1, P]], channel_multiplier=1))
                        then(nc.gpsimd.memset(u[:, :, 0:2], 0.0))
                        nc.gpsimd.memset(ones_bf[:, :], 1.0).then_inc(const_ready, 1)
                        then(nc.gpsimd.memset(future_big[:, :], 0.0))
                        then(nc.gpsimd.affine_select(out=future_big[:, :], in_=future_big[:, :], compare_op=ALU.is_ge,
                                                     fill=BIG, base=0, pattern=[[1, P]], channel_multiplier=-1))
                        then(nc.gpsimd.memset(before[:, :], 1.0))
                        then(nc.gpsimd.affine_select(out=before[:, :], in_=before[:, :], compare_op=ALU.is_ge,
                                                     fill=0.0, base=-1, pattern=[[1, P]], channel_multiplier=-1))
                        iota_f = lambda o, pat, base, cm: then(nc.gpsimd.iota(
                            o, pattern=pat, base=base, channel_multiplier=cm, allow_small_or_imprecise_dtypes=True))
                        iota_f(row_of_block[:, :], [[1, BLK]], 0, 0)
                        iota_f(expert_base[:, :], [[BLK, N_EXPERTS]], 0, 0)
                        iota_f(down_from_32[:, :], [[-1, N_EXPERTS]], N_EXPERTS, 0)
                        iota_f(tok_code[:, :, 0:1], [[2 * P, TT], [0, 1]], 0, 0)
                        iota_f(tok_code[:, :, 1:2], [[0, TT], [0, 1]], 0, 2)
                        then(nc.gpsimd.memset(both_halves[:, :, :], 0.0))
                        for j in range(2):
                            half = both_halves[:, j, :].rearrange("p (h r) -> p h r", h=2)
                            then(nc.gpsimd.affine_select(out=half, in_=half, compare_op=ALU.not_equal, fill=1.0,
                                                         base=-64 * j, pattern=[[0, 2], [-1, 64]], channel_multiplier=1))
                        then(nc.gpsimd.memset(eps_col[:, :], LN_EPS))
                        then(nc.gpsimd.memset(half_of_row[0:64, :], 0.0))
                        nc.gpsimd.memset(half_of_row[64:128, :], 1.0).then_inc(const_ready, 1)

                    @block.sync
                    def _(sp):
                        sp.dma_start(mem_sb, mem[0].rearrange("(t p) d -> p t d", p=P)).then_inc(in_mem, 16)
                        sp.dma_start(wkv[0], w_kv_mem[0].rearrange("(k p) n -> p k n", p=P)).then_inc(in_kv[0], 16)
                        sp.dma_start(x_sb[:, :, :], x[0].rearrange("(t p) d -> p t d", p=P)).then_inc(in_x, 16)

                        def load_slab(f):
                            if f >= 2:
                                sp.wait_ge(w_lo_ready, pieces.index(("bg", f - 2)) + 1)
                            for j in (1, 2, 0):
                                c = j * MIX_W + f * P
                                sp.dma_start(slab[f % 2][:, :, j, :], conv_w_in[0][:, c:c + P].rearrange(
                                    "(k p) n -> p k n", p=P)).then_inc(in_slab[f % 2], 16)
                        load_slab(0)
                        sp.dma_start(conv_taps[:, :, :], conv_w[0].rearrange("j (f p) -> p j f", p=P), allow_slow_non_contiguous=True).then_inc(in_small, 16)
                        sp.dma_start(router_sb[:, :, :], router_w.rearrange("(k p) n -> p k n", p=P)).then_inc(in_small, 16)
                        sp.dma_start(router_bias[:, :], router_b.unsqueeze(0).broadcast_to([P, N_EXPERTS])).then_inc(in_small, 16)
                        sp.dma_start(norm_g_sb[:, :], mlstm_norm_g[0].rearrange("(h p) -> p h", p=P), allow_slow_non_contiguous=True).then_inc(in_small, 16)
                        for j in range(2):
                            sp.dma_start(gate_bias[32 * j:32 * j + ML_HEADS, :],
                                         mlstm_gate_b[0][j * ML_HEADS:(j + 1) * ML_HEADS].unsqueeze(1)).then_inc(in_small, 16)
                        sp.wait_ge(copied, 4)
                        sp.dma_start(wqm, conv_w_in[0][:, 3 * MIX_W:].rearrange("(k p) n -> p k n", p=P)).then_inc(in_qm, 16)
                        sp.dma_start(wkv[1], w_kv_mem[1].rearrange("(k p) n -> p k n", p=P)).then_inc(in_kv[1], 16)
                        load_slab(1)
                        load_slab(2)
                        sp.wait_ge(projected, 4)
                        sp.dma_start(w_out_sb, w_out[0].rearrange("(k p) n -> p k n", p=P)).then_inc(in_w_out[0], 16)
                        for f in range(3, MIX_W // P):
                            load_slab(f)

                    @block.tensor
                    def _(pe):
                        pe.wait_ge(const_ready, 1)
                        groups = n = 0
                        for st in script:
                            kind = st[0]
                            if kind in ("tm", "tx"):
                                if st == ("tm", 0):
                                    pe.wait_ge(in_mem, 16)
                                if st == ("tx", 0):
                                    pe.wait_ge(in_x, 16)
                                if groups >= 6:
                                    pe.wait_ge(x_ready, groups - 5)
                                elif groups >= 2:
                                    pe.wait_ge(copied, groups - 1)
                                for j in range(4):
                                    if kind == "tm":
                                        src = mem_sb[:, j % 2, (2 * st[1] + j // 2) * P:(2 * st[1] + j // 2 + 1) * P]
                                    else:
                                        src = x_sb[:, j, st[1] * P:(st[1] + 1) * P]
                                    last = nc.tensor.transpose(bank[groups % 2][:, j * P:(j + 1) * P], src, ident[:, :])
                                last.then_inc(turned, 1)
                                groups += 1
                            elif kind in ("S", "T", "V"):
                                if st == ("S", 0):
                                    evacuated(pe, units.index(("qm", 1)))
                                att.pe(pe, kind, st[1])
                            else:
                                if n >= UB:
                                    evacuated(pe, n - UB)
                                o = bank[2 + n % UB]
                                if st == ("km", 0, 0):
                                    pe.wait_ge(in_kv[0], 16)
                                    pe.wait_ge(copied, 4)
                                if st == ("km", 1, 0):
                                    pe.wait_ge(in_kv[1], 16)
                                if st == ("cg", 0):
                                    pe.wait_ge(x_ready, KT)
                                if st in pieces:
                                    i = pieces.index(st)
                                    pe.wait_ge(w_lo_ready, i + 1)
                                for k in range(KT):
                                    fl = dict(start=(k == 0), stop=(k == KT - 1))
                                    if kind == "km":
                                        last = nc.tensor.matmul(o[:, 0:256], wkv[st[1]][:, k, st[2] * P:(st[2] + 1) * P],
                                                                memT[:, k, :], **fl)
                                    elif kind == "vm":
                                        last = nc.tensor.matmul(o[:, 0:256], memT[:, k, st[2] * P:(st[2] + 1) * P],
                                                                wkv[st[1]][:, k, 256:512], **fl)
                                    else:
                                        (w_hi, w_lo), (x_hi, x_lo) = w_half[i % 3], x_half
                                        for w, xh in ((w_hi, x_hi), (w_hi, x_lo), (w_lo, x_hi)):
                                            last = nc.tensor.matmul(o[:, :], w[:, k, :], xh[:, k, :],
                                                                    start=(k == 0 and w is w_hi and xh is x_hi),
                                                                    stop=(k == KT - 1 and w is w_lo))
                                last.then_inc(projected, 1)
                                n += 1

                    @block.scalar
                    def _(act):
                        groups = n = 0
                        for st in split_script:
                            kind = st[0]
                            if kind == "W":
                                raw = raw_weights(act, st[1])
                                place_free(act, st[1])
                                nc.scalar.copy(w_half[st[1] % 3][0][:, :, :], raw).then_inc(w_hi_ready, 1)
                            elif kind in ("tm", "tx"):
                                act.wait_ge(turned, groups + 1)
                                dst = (memT[:, 2 * st[1]:2 * st[1] + 2, :].rearrange("p k m -> p (k m)")
                                       if kind == "tm" else x_half[0][:, st[1], :])
                                nc.scalar.copy(dst, bank[groups % 2][:, :]).then_inc(copied, 1)
                                groups += 1
                            elif kind in ("S", "T", "V"):
                                att.act(act, kind, st[1])
                            else:
                                if kind in on_act:
                                    act.wait_ge(projected, n + 1)
                                    o = bank[2 + n % UB]
                                    if kind == "km":
                                        dst, o = (kmT0, kmT)[st[1]][:, st[2], :], o[:, 0:256]
                                    elif kind == "vm":
                                        dst, o = (vm0, vm)[st[1]][:, st[2], :], o[:, 0:256]
                                    elif kind == "qm":
                                        dst, o = qmT[:, st[1], :], o[:, :]
                                    else:
                                        dst, o = cgate[:, st[1] % 2, :], o[:, :]
                                        if st[1] >= 2:
                                            act.wait_ge(by_dve, 2 * st[1] - 3)
                                    nc.scalar.copy(dst, o).then_inc(by_act, 1)
                                n += 1
                        
                    @block.vector
                    def _(dve):
                        dve_chain.bind(dve)
                        then = dve_chain.then
                        n = 0
                        dve.wait_ge(const_ready, 1)
                        dve.wait_ge(in_small, 96)
                        for st in split_script:
                            kind = st[0]
                            if kind == "W":
                                raw, (hi, lo) = raw_weights(dve, st[1]), w_half[st[1] % 3]
                                dve.wait_ge(w_hi_ready, st[1] + 1)
                                nc.vector.tensor_tensor(lo[:, :, :], raw, hi[:, :, :], ALU.subtract).then_inc(w_lo_ready, 1)
                            elif kind == "tx":
                                k = st[1]
                                dve.wait_ge(copied, 5 + k)
                                nc.vector.tensor_tensor(x_half[1][:, k, :], bank[k % 2][:, :], x_half[0][:, k, :],
                                                        ALU.subtract).then_inc(x_ready, 1)
                            elif kind in ("S", "T", "V"):
                                att.dve(dve, kind, st[1])
                            elif kind in ("xin", "bg"):
                                dve.wait_ge(projected, n + 1)
                                f, o = st[1], bank[2 + n % UB]
                                ub, cb = u[:, f % 2, :], cv[:, f % 2, :]
                                if kind == "xin":
                                    evacuated(dve, n - 1)
                                    ins = nc.vector.tensor_tensor(ub[:, 2:SEQ + 2], cgate[:, f % 2, :], o[:, :], ALU.mult)
                                    ins.then_inc(by_dve, 1)
                                    dve.wait_ge(by_dve, 2 * f + 1)
                                    then(nc.vector.tensor_scalar(cb, ub[:, 0:SEQ], conv_taps[:, 0, f:f + 1], None, ALU.mult))
                                    for j in (1, 2):
                                        then(nc.vector.scalar_tensor_tensor(cb, ub[:, j:SEQ + j], conv_taps[:, j, f:f + 1],
                                                                            cb, ALU.mult, ALU.add))
                                else:
                                    nc.vector.tensor_tensor(headsT[:, f, :], cb, o[:, :], ALU.mult).then_inc(by_dve, 1)
                                    dve.wait_ge(by_dve, 2 * f + 2)
                            if kind in [z[0] for z in units]:
                                n += 1


        def route_memory(l, at):
            names = (("score", TT, N_EXPERTS), ("one", TT, 2, N_EXPERTS), ("slot_f", TT, 2), ("place", TT, N_EXPERTS),
                     ("near", TT, N_EXPERTS), ("gated", TT, 2, N_EXPERTS), ("both", TT, 2, N_EXPERTS), ("total", TT, 1),
                     ("raw_gates", TT, 2))
            return {n: sb(f"{n}_{l}", [P, *dims], at=at) for n, *dims in names}

        def gates_and_slots(mem_l):
            V, then = nc.vector, dve_chain.then
            score, one, slot_f, place, near, gated, both, total, raw_gates = (mem_l[n] for n in (
                "score", "one", "slot_f", "place", "near", "gated", "both", "total", "raw_gates"))
            pair_of = lambda a: a[:, :, :].unsqueeze(2).broadcast_to([P, TT, 2, N_EXPERTS])
            then(V.tensor_tensor(both[:, :, :, :], pair_of(score), one[:, :, :, :], ALU.mult))
            then(V.tensor_reduce(raw_gates[:, :, :], both[:, :, :, :], AX.X, ALU.add))
            then(V.tensor_reduce(total[:, :, :], raw_gates[:, :, :], AX.X, ALU.add))
            then(V.reciprocal(total[:, :, :], total[:, :, :]))
            then(V.tensor_tensor(raw_gates[:, :, :], raw_gates[:, :, :], total[:, :, :].broadcast_to([P, TT, 2]), ALU.mult))
            then(V.tensor_tensor(gated[:, :, :, :], one[:, :, :, :],
                                 raw_gates[:, :, :].unsqueeze(3).broadcast_to([P, TT, 2, N_EXPERTS]), ALU.mult))
            then(V.tensor_tensor(gate_of_expert[:, :, :], gated[:, :, 0, :], gated[:, :, 1, :], ALU.add))
            V.scalar_tensor_tensor(place[:, :, :], pos_or_none[:, :, :], float(BLK - 1),
                                   expert_base[:, :].unsqueeze(1).broadcast_to([P, TT, N_EXPERTS]), ALU.min, ALU.add)
            then(V.tensor_scalar(near[:, :, :], pos_or_none[:, :, :], float(BLK), None, ALU.is_lt))
            V.tensor_tensor(both[:, :, :, :], pair_of(place), one[:, :, :, :], ALU.mult)
            then(V.tensor_tensor(gated[:, :, :, :], pair_of(near), gated[:, :, :, :], ALU.mult))
            V.tensor_reduce(gates[:, :, :], gated[:, :, :, :], AX.X, ALU.add)
            then(V.tensor_reduce(slot_f[:, :, :], both[:, :, :, :], AX.X, ALU.add))
            then(V.tensor_copy(slots[:, :, :], slot_f[:, :, :]))

        def out_and_route_phase(l, mem_l):
            ph = ExitStack()
            ph.callback(end_phase)
            with ph:
                s = lambda n: sem(f"{n}_{l}", ph)
                score, one = mem_l["score"], mem_l["one"]
                most = sb(f"most_{l}", [P, 1], at=ph)
                ln_g, ln_b = sb(f"ln1_g_{l}", [P, D_MODEL], at=ph), sb(f"ln1_b_{l}", [P, D_MODEL], at=ph)
                once = lambda n, *d: sb(f"{n}_{l}", [P, *d], at=ph)
                sel, work = (once(n, 2, N_EXPERTS) for n in ("sel", "work"))
                hi1, lo1, hi2, lo2, gsum, gwork = (once(n, 2, N_GROUPS) for n in ("hi1", "lo1", "hi2", "lo2", "gsum", "gwork"))
                top = once("top", 2, 1)
                taken = sb(f"taken_{l}", [P, TT, N_EXPERTS], BF16, at=ph)
                idx_f = sb(f"idx_f_{l}", [P, N_EXPERTS // 2], at=ph)
                onehot = sb(f"onehot_{l}", [P, 2, N_EXPERTS, BLK], BF16, at=ph)
                in_ln, out_done, summed, normed = s("p1_in_ln"), s("p1_out"), s("p1_sum"), s("p1_normed")
                turned, copied, routed, scored = s("p1_turned"), s("p1_copied"), s("p1_routed"), s("p1_scored")
                chosen, counted, marked, coded, code_read, spread_out, stored = (
                    s("p1_" + n) for n in ("chosen", "counted", "marked", "coded", "code_read", "spread_out", "stored"))
                var_ready, std_ready, scaled = s("p1_var"), s("p1_std"), s("p1_scaled")

                script = [("O", 0), ("O", 2), ("O", 3), ("T", 0), ("O", 4), ("R", 0), ("O", 5), ("T", 1),
                          ("O", 6), ("R", 1), ("O", 7), ("T", 2), ("R", 2), ("P", 0), ("T", 3), ("R", 3), ("C", 0),
                          ("C", 1), ("P", 1), ("C", 2), ("C", 3)]
                POS_BANK, CODE_BANK = (bank[7], bank[0]), bank[1]
                hi_ready, lo_ready = s("p1_hi"), s("p1_lo")
                w_half = halves_at(f"w_out_half_{l}", [P, KT, D_MODEL], ring_at + 4 * W_EXP, ring_at + 4 * 2 * W_EXP)
                h_half = halves_at(f"heads_half_{l}", [P, KT, SEQ], ring_at + 4 * (W_EXP + 8192),
                                   ring_at + 4 * (2 * W_EXP + 8192))
                with nc.Block() as block:
                    @block.sync
                    def _(sp):
                        for row, dst in ((ln1_g, ln_g), (ln1_b, ln_b)):
                            sp.dma_start(dst[:, :], row[l].unsqueeze(0).broadcast_to([P, D_MODEL])).then_inc(in_ln, 16)
                        load_gate_up(sp, l, 0, 0, in_gu[l][0])
                        load_down(sp, l, 0, 0, in_dn[l][0])
                        for t in range(TT):
                            if t == TT - 1:
                                sp.wait_ge(out_done, 2 * TT)
                                load_gate_up(sp, l, 1, 1, in_gu[l][1])
                            sp.wait_ge(normed, t + 1)
                            sp.dma_start(x1_dram[l].rearrange("(t p h) d -> p t (h d)", t=TT, h=2)[:, t, :],
                                         x_sb[:, t, :]).then_inc(stored, 16)
                        load_down(sp, l, 1, 1, in_dn[l][1])
                        load_gate_up(sp, l, 2, 2, in_gu[l][2])
                        sp.wait_ge(stored, 16 * TT)

                    @block.gpsimd
                    def _(pool):
                        add_biases(pool, ln_b, in_ln, scaled, normed)

                    @block.tensor
                    def _(pe):
                        def project(t, n, k):
                            w, h = (a[:, k, n * 512:(n + 1) * 512] for a in w_half), (a[:, k, t * P:(t + 1) * P] for a in h_half)
                            (w_hi, w_lo), (h_hi, h_lo) = w, h
                            for i, (a, b) in enumerate(((h_hi, w_hi), (h_lo, w_hi), (h_hi, w_lo))):
                                last = nc.tensor.matmul(bank[2 * (t % 2) + n][:, :], a, b, start=(k == 0 and i == 0),
                                                        stop=(k == KT - 1 and i == 2))
                            if k == KT - 1:
                                last.then_inc(out_done, 1)

                        for kind, t in script:
                            if kind == "O":
                                if t >= 4:
                                    pe.wait_ge(summed, t - 3)
                                for k in range(KT):
                                    if t == 0:
                                        pe.wait_ge(lo_ready, k + 1)
                                        project(0, 0, k)
                                        project(0, 1, k)
                                    else:
                                        project(t // 2, t % 2, k)
                            elif kind == "T":
                                pe.wait_ge(normed, t + 1)
                                for b in range(2):
                                    if t:
                                        pe.wait_ge(copied, 2 * t - 1 + b)
                                    for j in range(4):
                                        k = 4 * b + j
                                        last = nc.tensor.transpose(bank[4 + b][:, j * P:(j + 1) * P],
                                                                   x_sb[:, t, k * P:(k + 1) * P], ident[:, :])
                                    last.then_inc(turned, 1)
                            elif kind == "R":
                                if t:
                                    pe.wait_ge(scored, t)
                                for k in range(KT):
                                    if k % 4 == 0:
                                        pe.wait_ge(copied, 2 * t + k // 4 + 1)
                                    last = nc.tensor.matmul(bank[6][:, t * 32:(t + 1) * 32], xT[:, k, t * P:(t + 1) * P],
                                                            router_sb[:, k, :], start=(k == 0), stop=(k == KT - 1))
                                last.then_inc(routed, 1)
                            elif kind == "P":
                                o = POS_BANK[t]
                                pe.wait_ge(chosen, t + 1)
                                if t:
                                    pe.wait_ge(summed, 6)
                                for j in range(2):
                                    tile = 2 * t + j
                                    for q in range(tile + 1):
                                        last = nc.tensor.matmul(o[:, 32 * j:32 * j + 32],
                                                                before[:, :] if q == tile else ones_bf[:, :],
                                                                taken[:, q, :], start=(q == 0), stop=(q == tile))
                                if t:
                                    for q in range(TT):
                                        last = nc.tensor.matmul(o[:, 64:96], ones_bf[:, :], taken[:, q, :],
                                                                start=(q == 0), stop=(q == TT - 1))
                                last.then_inc(counted, 1)
                            else:
                                pe.wait_ge(marked, t + 1)
                                if t == 0:
                                    pe.wait_ge(summed, 6)
                                for pair in range(N_EXPERTS // 2):
                                    last = nc.tensor.matmul(CODE_BANK[:, 8 * pair + 2 * t:8 * pair + 2 * t + 2],
                                                            onehot[:, t % 2, 2 * pair:2 * pair + 2, :].rearrange("p e r -> p (e r)"),
                                                            tok_code[:, t, :], start=True, stop=True)
                                last.then_inc(coded, 1)
                        pe.wait_ge(code_read, 1)
                        for j in range(2):
                            last = nc.tensor.matmul(bank[4][:, 16 * j:16 * j + 16], both_halves[:, j, :], idx_f[:, :],
                                                    start=True, stop=True)
                        last.then_inc(spread_out, 1)

                    @block.scalar
                    def _(act):
                        act.wait_ge(in_w_out[l], 16)
                        for k in range(KT):
                            nc.scalar.copy(w_half[0][:, k, :], w_out_sb[:, k, :])
                            nc.scalar.copy(h_half[0][:, k, :], headsT[:, k, :]).then_inc(hi_ready, 1)
                        for kind, t in [("L", 0), ("L", 1), ("T", 0), ("R", 0), ("L", 2), ("T", 1), ("R", 1), ("T", 2),
                                        ("R", 2), ("L", 3), ("T", 3), ("R", 3)]:
                            if kind == "L":
                                std_of_tile(act, t, var_ready, std_ready)
                            elif kind == "T":
                                for b in range(2):
                                    act.wait_ge(turned, 2 * t + b + 1)
                                    nc.scalar.copy(xT[:, 4 * b:4 * b + 4, t * P:(t + 1) * P],
                                                   bank[4 + b][:, :].rearrange("p (k s) -> p k s", k=4)).then_inc(copied, 1)
                            elif kind == "R":
                                act.wait_ge(routed, t + 1)
                                nc.scalar.activation(score[:, t, :], bank[6][:, t * 32:(t + 1) * 32],
                                                     ACT.Sigmoid).then_inc(scored, 1)

                    @block.vector
                    def _(dve):
                        dve_chain.bind(dve)
                        then = dve_chain.then
                        V = nc.vector
                        order = down_from_32[:, :].unsqueeze(1).broadcast_to([P, 2, N_EXPERTS])
                        g_order = down_from_32[:, 0:N_GROUPS].unsqueeze(1).broadcast_to([P, 2, N_GROUPS])

                        def residual_and_norm(t):
                            for n in range(2):
                                dve.wait_ge(out_done, 2 * t + n + 1)
                                half = x_sb[:, t, n * 512:(n + 1) * 512]
                                V.scalar_tensor_tensor(half, half, ALPHA, bank[2 * (t % 2) + n][:, :],
                                                       ALU.mult, ALU.add).then_inc(summed, 1)
                            dve.wait_ge(summed, 2 * t + 2)
                            layer_norm(dve, t, ln_g, ln_b, var_ready, std_ready, scaled, normed)

                        def first_of_max(values, w, o, hot, width):
                            over = top[:, :, :].broadcast_to([P, 2, width])
                            then(V.tensor_reduce(top[:, :, :], values, AX.X, ALU.max))
                            then(V.tensor_tensor(w, values, over, ALU.is_equal))
                            then(V.tensor_tensor(w, w, o, ALU.mult))
                            then(V.tensor_reduce(top[:, :, :], w, AX.X, ALU.max))
                            then(V.tensor_tensor(hot, over, o, ALU.is_equal))

                        def choose(h):
                            z = slice(2 * h, 2 * h + 2)
                            dve.wait_ge(scored, 2 * h + 2)
                            then(V.tensor_tensor(sel[:, :, :], score[:, z, :],
                                                 router_bias[:, :].unsqueeze(1).broadcast_to([P, 2, N_EXPERTS]), ALU.add))
                            m = sel[:, :, :].rearrange("p t (g j) -> p t g j", j=PER_GROUP)
                            V.tensor_tensor(hi1[:, :, :], m[:, :, :, 0], m[:, :, :, 1], ALU.max)
                            V.tensor_tensor(lo1[:, :, :], m[:, :, :, 0], m[:, :, :, 1], ALU.min)
                            V.tensor_tensor(hi2[:, :, :], m[:, :, :, 2], m[:, :, :, 3], ALU.max)
                            then(V.tensor_tensor(lo2[:, :, :], m[:, :, :, 2], m[:, :, :, 3], ALU.min))
                            V.tensor_tensor(gsum[:, :, :], hi1[:, :, :], hi2[:, :, :], ALU.max)
                            V.tensor_tensor(gwork[:, :, :], hi1[:, :, :], hi2[:, :, :], ALU.min)
                            then(V.tensor_tensor(lo2[:, :, :], lo1[:, :, :], lo2[:, :, :], ALU.max))
                            then(V.tensor_tensor(gwork[:, :, :], gwork[:, :, :], lo2[:, :, :], ALU.max))
                            then(V.tensor_tensor(gsum[:, :, :], gsum[:, :, :], gwork[:, :, :], ALU.add))
                            first_of_max(gsum[:, :, :], gwork[:, :, :], g_order, hi2[:, :, :], N_GROUPS)
                            spread = lambda a: a[:, :, :].unsqueeze(3).broadcast_to([P, 2, N_GROUPS, PER_GROUP])
                            V.tensor_scalar(lo2[:, :, :], hi2[:, :, :], BIG, -BIG, ALU.mult, ALU.add)
                            then(V.tensor_tensor(m, m, spread(hi2), ALU.mult))
                            then(V.tensor_tensor(m, m, spread(lo2), ALU.add))
                            first_of_max(sel[:, :, :], work[:, :, :], order, one[:, z, 0, :], N_EXPERTS)
                            then(V.scalar_tensor_tensor(sel[:, :, :], one[:, z, 0, :], -BIG, sel[:, :, :], ALU.mult, ALU.add))
                            first_of_max(sel[:, :, :], work[:, :, :], order, one[:, z, 1, :], N_EXPERTS)
                            V.tensor_tensor(taken[:, z, :], one[:, z, 0, :], one[:, z, 1, :], ALU.add).then_inc(chosen, 1)

                        def place(h):
                            z = slice(2 * h, 2 * h + 2)
                            dve.wait_ge(counted, h + 1)
                            pos = POS_BANK[h][:, 0:64].rearrange("p (t e) -> p t e", t=2)
                            then(V.scalar_tensor_tensor(pos_or_none[:, z, :], pos, 1.0, taken[:, z, :], ALU.add, ALU.mult))
                            then(V.tensor_scalar(pos_or_none[:, z, :], pos_or_none[:, z, :], -1.0, None, ALU.add))
                            for t in (2 * h, 2 * h + 1):
                                if t >= 2:
                                    dve.wait_ge(coded, t - 1)
                                V.tensor_tensor(onehot[:, t % 2, :, :],
                                                pos_or_none[:, t, :].unsqueeze(2).broadcast_to([P, N_EXPERTS, BLK]),
                                                row_of_block[:, :].unsqueeze(1).broadcast_to([P, N_EXPERTS, BLK]),
                                                ALU.is_equal).then_inc(marked, 1)

                        dve.wait_ge(in_w_out[l], 16)
                        for k in range(KT):
                            dve.wait_ge(hi_ready, k + 1)
                            V.tensor_tensor(w_half[1][:, k, :], w_out_sb[:, k, :], w_half[0][:, k, :], ALU.subtract)
                            V.tensor_tensor(h_half[1][:, k, :], headsT[:, k, :], h_half[0][:, k, :],
                                            ALU.subtract).then_inc(lo_ready, 1)
                        dve.wait_ge(in_ln, 32)
                        for t in range(3):
                            residual_and_norm(t)
                        choose(0)
                        residual_and_norm(3)
                        place(0)
                        choose(1)
                        place(1)
                        dve.wait_ge(coded, TT)
                        V.tensor_reduce(idx_f[:, :], CODE_BANK[:, 0:128].rearrange("p (e c) -> p e c", c=2 * TT),
                                        AX.X, ALU.add).then_inc(code_read, 1)
                        then(V.tensor_reduce(most[:, :], POS_BANK[1][:, 64:96], AX.X, ALU.max))
                        then(V.tensor_copy(most_rows[0:1, 0:1], most[0:1, :]))
                        dve.wait_ge(spread_out, 1)
                        then(V.tensor_scalar(block_rows[:, :].rearrange("p (e j) -> p j e", j=2),
                                             bank[4][:, 0:32].rearrange("p (j e) -> p j e", j=2),
                                             half_of_row[:, :], None, ALU.add))


        def expert_phase(l, mem_l):
            ph = ExitStack()
            ph.callback(end_phase)
            with ph:
                s = lambda n: sem(f"{n}_{l}", ph)
                flat = xT[:, :, :].rearrange("p k s -> p (k s)")
                part = lambda i, n: flat[:, i:i + n]
                xg = [part(512 * i, 512) for i in range(3)]
                xgT = [part(1536 + 512 * i, 512).rearrange("p (c r) -> p c r", c=4) for i in range(3)]
                silu = [part(3072 + 256 * i, 256) for i in range(3)]
                hid = [sb(f"hid{i}_{l}", [P, 256], at=ph) for i in range(3)]
                hidT = [sb(f"hidT{i}_{l}", [P, 2, P], at=ph) for i in range(3)]
                y = [sb(f"y{i}_{l}", [P, 512], at=ph) for i in range(3)]
                gathered = [s(f"p2_gathered{i}") for i in range(3)]
                stored = [s(f"p2_stored{i}") for i in range(3)]
                xturned, xcopied, gu_done, activated, hid_done = (s("p2_" + n) for n in ("xturned", "xcopied", "gu_done", "activated", "hid_done"))
                hturned, hcopied, y_done, y_copied = (s("p2_" + n) for n in ("hturned", "hcopied", "y_done", "y_copied"))
                last_gu, last_dn = s("p2_last_gu"), s("p2_last_dn")
                X_BANK, H_BANK = bank[0], bank[1]
                GU_BANK, Y_BANK = bank[2:5], bank[5:8]

                with nc.Block() as block:
                    @block.sync
                    def _(sp):
                        def load(e, r):
                            sp.wait_ge(gu_done, e - 2)
                            load_gate_up(sp, l, e, r, in_gu[l][r])
                            sp.wait_ge(y_done, e - 2)
                            load_down(sp, l, e, r, in_dn[l][r])
                        sp.wait_ge(gathered[0], 16)
                        load_down(sp, l, 2, 2, in_dn[l][2])
                        with sp.Fori(0, 9) as i:
                            for r in range(3):
                                load(3 * i + (3 + r), r)
                        load(30, 0)
                        e = N_EXPERTS - 1
                        gu, dn = expert_views(1)
                        sp.wait_ge(gu_done, e - 2)
                        for h in range(2):
                            for m, w in ((0, w_gate), (1, w_up)):
                                sp.dma_start(gu[:, m, h], w[l, e, 512 * h:512 * h + 512].rearrange("(p c) f -> p c f", p=P)
                                             ).then_inc((in_gu[l][1], last_gu)[h], 16)
                        sp.wait_ge(y_done, e - 2)
                        for f in range(2):
                            sp.dma_start(dn[:, f], w_down[l, e, 256 * f:256 * f + 256].rearrange("(p c) d -> p c d", p=P)
                                         ).then_inc((in_dn[l][1], last_dn)[f], 16)

                    @block.gpsimd
                    def _(pool):
                        for e in range(N_EXPERTS):
                            if e >= 3:
                                pool.wait_ge(xturned, e - 2)
                            nc.gpsimd.indirect_dma_start(xg[e % 3], None, x1_dram[l],
                                                         bass.IndirectOffsetOnAxis(ap=block_rows[:, e:e + 1], axis=0)
                                                         ).then_inc(gathered[e % 3], 16)

                    @block.tensor
                    def _(pe):
                        def turn_rows(e, j, count):
                            pe.wait_ge(gathered[j], 16 * count)
                            if not (isinstance(e, int) and e == 0):
                                pe.wait_ge(xcopied, e)
                            for c in range(4):
                                last = nc.tensor.transpose(X_BANK[:, c * P:(c + 1) * P], xg[j][:, c::4], ident[:, :])
                            last.then_inc(xturned, 1)

                        def gate_up(e, j, count, first=False, halved=False):
                            pe.wait_ge(in_gu[l][j], 32 * count)
                            pe.wait_ge(xcopied, e + 1)
                            if not first:
                                pe.wait_ge(hid_done, e - 2)
                            gu, _ = expert_views(j)
                            for h in range(2):
                                if h and halved:
                                    pe.wait_ge(last_gu, 32)
                                for c in range(4):
                                    for f in range(2):
                                        last = nc.tensor.matmul(GU_BANK[j][64 * f:64 * f + 64, :], xgT[j][:, c, 64 * h:64 * h + 64],
                                                                gu[:, :, h, c, 256 * f:256 * f + 256],
                                                                start=(h == 0 and c == 0), stop=(h == 1 and c == 3))
                            last.then_inc(gu_done, 1)

                        def turn_hidden(e, j):
                            pe.wait_ge(hid_done, e + 1)
                            if not (isinstance(e, int) and e == 0):
                                pe.wait_ge(hcopied, e)
                            for c in range(2):
                                last = nc.tensor.transpose(H_BANK[:, c * P:(c + 1) * P], hid[j][:, c::2], ident[:, :])
                            last.then_inc(hturned, 1)

                        def down(e, j, count, first=False, halved=False):
                            pe.wait_ge(in_dn[l][j], 16 * count)
                            pe.wait_ge(hcopied, e + 1)
                            if not first:
                                pe.wait_ge(y_copied, e - 1)
                            _, dn = expert_views(j)
                            for f in range(2):
                                if f and halved:
                                    pe.wait_ge(last_dn, 16)
                                for c in range(2):
                                    for n in range(2):
                                        last = nc.tensor.matmul(Y_BANK[j][64 * n:64 * n + 64, :], hidT[j][:, c, 64 * f:64 * f + 64],
                                                                dn[:, f, c, 512 * n:512 * n + 512],
                                                                start=(f == 0 and c == 0), stop=(f == 1 and c == 1))
                            last.then_inc(y_done, 1)

                        turn_rows(0, 0, 1)
                        for e in range(3):
                            gate_up(e, e, 1, first=True)
                            turn_rows(e + 1, (e + 1) % 3, (e + 1) // 3 + 1)
                            if e:
                                down(e - 1, e - 1, 1, first=True)
                            turn_hidden(e, e)
                        with pe.Fori(0, 9) as i:
                            for j in range(3):
                                e = 3 * i + (3 + j)
                                gate_up(e, j, i + 2)
                                turn_rows(e + 1, (j + 1) % 3, i + (2 if j < 2 else 3))
                                down(e - 1, (j + 2) % 3, i + (2 if j else 1))
                                turn_hidden(e, j)
                        down(29, 2, 10)
                        gate_up(30, 0, 11)
                        turn_rows(31, 1, 11)
                        turn_hidden(30, 0)
                        down(30, 0, 11)
                        gate_up(31, 1, 11, halved=True)
                        turn_hidden(31, 1)
                        down(31, 1, 11, halved=True)

                    @block.scalar
                    def _(act):
                        def activate(e, j, first=False):
                            act.wait_ge(gu_done, e + 1)
                            if not first:
                                act.wait_ge(hid_done, e - 2)
                            nc.scalar.activation(silu[j], GU_BANK[j][:, 0:256], ACT.Silu).then_inc(activated, 1)

                        def put_out(e, j, count, first=False):
                            act.wait_ge(y_done, e + 1)
                            if not first:
                                act.wait_ge(stored[j], 32 * (count - 1))
                            nc.scalar.copy(y[j][:, :], Y_BANK[j][:, :]).then_inc(y_copied, 1)
                            act.wait_ge(y_copied, e + 1)
                            for n in range(2):
                                act.dma_start(y_dram[l][bass.ds(e * BLK, BLK), 512 * n:512 * n + 512],
                                              y[j][64 * n:64 * n + 64, :]).then_inc(stored[j], 16)

                        for e in range(3):
                            activate(e, e, first=True)
                            if e:
                                put_out(e - 1, e - 1, 1, first=True)
                        activate(3, 0)
                        put_out(2, 2, 1, first=True)
                        with act.Fori(0, 9) as i:
                            for j in range(3):
                                activate(3 * i + (4 + j), (1 + j) % 3)
                                put_out(3 * i + (3 + j), j, i + 2)
                        put_out(30, 0, 11)
                        activate(31, 1)
                        put_out(31, 1, 11)
                        act.wait_ge(stored[0], 32 * 11)
                        act.wait_ge(stored[1], 32 * 11)
                        act.wait_ge(stored[2], 32 * 10)

                    @block.vector
                    def _(dve):
                        def rows_in(e, j, first=False):
                            dve.wait_ge(xturned, e + 1)
                            if not first:
                                dve.wait_ge(gu_done, e - 2)
                            nc.vector.tensor_copy(xgT[j].rearrange("p c r -> p (c r)"), X_BANK[:, :]).then_inc(xcopied, 1)

                        def hidden(e, j, first=False):
                            dve.wait_ge(activated, e + 1)
                            if not first:
                                dve.wait_ge(hturned, e - 2)
                            nc.vector.tensor_tensor(hid[j][:, :], silu[j], GU_BANK[j][:, 256:512], ALU.mult).then_inc(hid_done, 1)
                            dve.wait_ge(hturned, e + 1)
                            if not first:
                                dve.wait_ge(y_done, e - 2)
                            nc.vector.tensor_copy(hidT[j][:, :, :].rearrange("p c r -> p (c r)"),
                                                  H_BANK[:, 0:256]).then_inc(hcopied, 1)

                        dve_chain.bind(dve)
                        rows_in(0, 0, first=True)
                        gates_and_slots(mem_l)
                        for e in range(3):
                            rows_in(e + 1, (e + 1) % 3, first=(e < 2))
                            hidden(e, e, first=True)
                        with dve.Fori(0, 9) as i:
                            for j in range(3):
                                e = 3 * i + (3 + j)
                                rows_in(e + 1, (j + 1) % 3)
                                hidden(e, j)
                        rows_in(31, 1)
                        hidden(30, 0)
                        hidden(31, 1)


        def later_blocks(l, ph):
            s = lambda n: sem(f"later_{n}_{l}", ph)
            take = lambda o, n: R1[:, 8192 + o:8192 + o + n]
            later_rows = take(0, BLK)
            mark = take(64, 128).bitcast(BF16).rearrange("p (t r) -> p t r", t=TT)
            gated = take(192, 256).rearrange("p (t r) -> p t r", t=TT)
            gated2 = take(448, 512).rearrange("p (t h r) -> p t h r", t=TT, h=2)
            gatedT = take(960, 512).rearrange("p (t k) -> p t k", t=TT)
            code, idx, no_rows, rows_idx = (take(1472 + i, 1).bitcast(U32) if i else take(1472, 1) for i in range(4))
            xg, xgT = take(1536, 512), take(2048, 512).rearrange("p (c r) -> p c r", c=4)
            silu, hid = take(2560, 256), take(2816, 256)
            hidT, y = take(3072, 256).rearrange("p (c r) -> p c r", c=2), take(3328, 512)
            moved, marked, coded, code_read, indexed, gathered = (
                s(n) for n in ("moved", "marked", "coded", "code_read", "indexed", "gathered"))
            gated_ready, xturned, xcopied, gu_done, activated, hid_done = (
                s(n) for n in ("gated", "xturned", "xcopied", "gu_done", "activated", "hid_done"))
            hturned, hcopied, y_done, y_copied, gturned, gcopied = (
                s(n) for n in ("hturned", "hcopied", "y_done", "y_copied", "gturned", "gcopied"))
            combined, added, in_gu1, in_dn1, gated_half, code_summed = (
                s(n) for n in ("combined", "added", "in_gu", "in_dn", "gated_half", "code_summed"))

            def turns(eng, step, begin=None):
                top = eng.value_load(most_rows[0:1, 0:1], min_val=0, max_val=SEQ)
                with eng.If(top > BLK):
                    with eng.Fori(1, SEQ // BLK) as b:
                        with eng.If(top > b * BLK):
                            if begin:
                                begin(b)
                            with eng.Fori(0, N_EXPERTS) as e:
                                step(e, (b - 1) * N_EXPERTS + e, b)
                            eng.nop()
                        with eng.Else():
                            eng.nop()
                    eng.nop()
                with eng.Else():
                    eng.nop()

            def later_sp(sp):
                def step(e, n, b):
                    sp.wait_ge(y_done, n + 1)
                    load_gate_up(sp, l, e, 2, in_gu1)
                    load_down(sp, l, e, 2, in_dn1)
                turns(sp, step)

            def later_pool(pool):
                def step(e, n, b):
                    pool.wait_ge(xturned, n + 1)
                    pool.wait_ge(code_read, n + 1)
                    nc.gpsimd.tensor_tensor(rows_idx, idx, no_rows, ALU.add).then_inc(indexed, 1)
                    pool.drain()
                    nc.gpsimd.indirect_dma_start(xg, None, x1_dram[l],
                                                 bass.IndirectOffsetOnAxis(ap=rows_idx, axis=0)).then_inc(gathered, 16)
                turns(pool, step)

            def later_pe(pe):
                def step(e, n, b):
                    pe.wait_ge(marked, n + 1)
                    for h in range(2):
                        for t in range(TT):
                            last = nc.tensor.matmul(bank[h][64 * h:64 * h + 64, 0:2], mark[:, t, :], tok_code[:, t, :],
                                                    start=(t == 0), stop=(t == TT - 1))
                    last.then_inc(coded, 1)
                    pe.wait_ge(gated_ready, n + 1)
                    for t in range(TT):
                        last = nc.tensor.transpose(bank[5][:, t * P:(t + 1) * P],
                                                   gated2[:, t, :, :].rearrange("p h r -> p (h r)"), ident[:, :])
                    last.then_inc(gturned, 1)
                    pe.wait_ge(gathered, 16 * (n + 1))
                    pe.wait_ge(code_read, n + 1)
                    for c in range(4):
                        last = nc.tensor.transpose(bank[1][:, c * P:(c + 1) * P], xg[:, c::4], ident[:, :])
                    last.then_inc(xturned, 1)
                    pe.wait_ge(xcopied, n + 1)
                    pe.wait_ge(in_gu1, 32 * (n + 1))
                    gu, dn = expert_views(2)
                    for h in range(2):
                        for c in range(4):
                            for f in range(2):
                                last = nc.tensor.matmul(bank[2][64 * f:64 * f + 64, :], xgT[:, c, 64 * h:64 * h + 64],
                                                        gu[:, :, h, c, 256 * f:256 * f + 256],
                                                        start=(h == 0 and c == 0), stop=(h == 1 and c == 3))
                    last.then_inc(gu_done, 1)
                    pe.wait_ge(hid_done, n + 1)
                    for c in range(2):
                        last = nc.tensor.transpose(bank[3][:, c * P:(c + 1) * P], hid[:, c::2], ident[:, :])
                    last.then_inc(hturned, 1)
                    pe.wait_ge(hcopied, n + 1)
                    pe.wait_ge(in_dn1, 16 * (n + 1))
                    for f in range(2):
                        for c in range(2):
                            for m in range(2):
                                last = nc.tensor.matmul(bank[4][64 * m:64 * m + 64, :], hidT[:, c, 64 * f:64 * f + 64],
                                                        dn[:, f, c, 512 * m:512 * m + 512],
                                                        start=(f == 0 and c == 0), stop=(f == 1 and c == 1))
                    last.then_inc(y_done, 1)
                    pe.wait_ge(gcopied, n + 1)
                    pe.wait_ge(y_copied, n + 1)
                    for t in range(TT):
                        pe.wait_ge(added, 4 * n + t + 1)
                        for m in range(2):
                            last = nc.tensor.matmul(bank[6 + m][:, :], gatedT[64 * m:64 * m + 64, t, :],
                                                    y[64 * m:64 * m + 64, :], start=True, stop=True)
                        last.then_inc(combined, 1)
                for free in (y_done, xturned, combined):
                    pe.sem_inc(free, 1)
                turns(pe, step)

            def later_act(act):
                def step(e, n, b):
                    act.wait_ge(gu_done, n + 1)
                    nc.scalar.activation(silu, bank[2][:, 0:256], ACT.Silu).then_inc(activated, 1)
                turns(act, step)

            def later_dve(dve):
                dve_chain.bind(dve)
                V = nc.vector
                dve.sem_inc(added, 1)
                V.memset(no_rows, 0)
                dve_chain.then(V.tensor_copy(later_rows, row_of_block[:, :]))

                def begin(b):
                    V.tensor_scalar(later_rows, later_rows, float(BLK), None, ALU.add).then_inc(moved, 1)

                def step(e, n, b):
                    col = lambda a: a[:, :, bass.ds(e, 1)].broadcast_to([P, TT, BLK])
                    dve.wait_ge(moved, b)
                    dve.wait_ge(combined, 4 * n + 1)
                    V.tensor_tensor(mark, col(pos_or_none), later_rows.unsqueeze(1).broadcast_to([P, TT, BLK]),
                                    ALU.is_equal).then_inc(marked, 1)
                    dve.wait_ge(marked, n + 1)
                    V.tensor_tensor(gated, mark, col(gate_of_expert), ALU.mult).then_inc(gated_half, 1)
                    dve.wait_ge(gated_half, n + 1)
                    V.tensor_scalar(gated2[:, :, 0, :], gated, 1.0 / ALPHA, None, ALU.mult)
                    V.tensor_scalar(gated2[:, :, 1, :], gated, 1.0 / ALPHA, None, ALU.mult).then_inc(gated_ready, 1)
                    dve.wait_ge(coded, n + 1)
                    V.tensor_reduce(code[0:64, :], bank[0][0:64, 0:2], AX.X, ALU.add)
                    V.tensor_reduce(code[64:128, :], bank[1][64:128, 0:2], AX.X, ALU.add).then_inc(code_summed, 1)
                    dve.wait_ge(code_summed, n + 1)
                    V.tensor_tensor(idx, code, half_of_row[:, :], ALU.add).then_inc(code_read, 1)
                    dve.wait_ge(gturned, n + 1)
                    V.tensor_copy(gatedT.rearrange("p t k -> p (t k)"), bank[5][:, :]).then_inc(gcopied, 1)
                    dve.wait_ge(xturned, n + 2)
                    V.tensor_copy(xgT.rearrange("p c r -> p (c r)"), bank[1][:, :]).then_inc(xcopied, 1)
                    dve.wait_ge(activated, n + 1)
                    V.tensor_tensor(hid, silu, bank[2][:, 256:512], ALU.mult).then_inc(hid_done, 1)
                    dve.wait_ge(hturned, n + 1)
                    V.tensor_copy(hidT.rearrange("p c r -> p (c r)"), bank[3][:, 0:256]).then_inc(hcopied, 1)
                    dve.wait_ge(y_done, n + 2)
                    V.tensor_copy(y, bank[4][:, :]).then_inc(y_copied, 1)
                    for t in range(TT):
                        dve.wait_ge(combined, 4 * n + t + 2)
                        for m in range(2):
                            part = x_sb[:, t, 512 * m:512 * m + 512]
                            last = V.tensor_tensor(part, part, bank[6 + m][:, :], ALU.add)
                        last.then_inc(added, 1)
                    dve.wait_ge(added, 4 * n + 5)
                turns(dve, step, begin)
            return later_sp, later_pool, later_pe, later_act, later_dve

        slabs = [(4 * MIX_W, 2 * ML_HEADS + XATT_W)] + [(512 * i, 512) for i in range(6)]
        slab = [R0[:, i * 4096:(i + 1) * 4096].rearrange("p (k n) -> p k n", k=KT) for i in range(2)]

        def load_mlstm_slab(sp, i):
            c, w = slabs[i]
            sp.dma_start(slab[i % 2][:, :, 0:w], mlstm_w_in[0][:, c:c + w].rearrange("(k p) n -> p k n", p=P)
                         ).then_inc(in_w[i % 2], 16)


        def combine_phase(l):
            ph = ExitStack()
            ph.callback(end_phase)
            last_layer = l == DEPTH - 1
            with ph:
                s = lambda n: sem(f"{n}_{l}", ph)
                ln_g, ln_b = sb(f"ln2_g_{l}", [P, D_MODEL], at=ph), sb(f"ln2_b_{l}", [P, D_MODEL], at=ph)
                later_sp, later_pool, later_pe, later_act, later_dve = later_blocks(l, ph)
                rows = R1[:, 0:8192].rearrange("p (i d) -> p i d", i=2 * TT)
                fetched = [s(f"p3_fetched{t}") for t in range(TT)]
                in_ln, normed, turned, copied, stored = (s("p3_" + n) for n in ("in_ln", "normed", "turned", "copied", "stored"))
                var_ready, std_ready, scaled, first_gated = s("p3_var"), s("p3_std"), s("p3_scaled"), s("p3_first")
                lo_ready, inverted, normalized = s("p3_lo_ready"), s("p3_inverted"), s("p3_normalized")
                by_tile = lambda a, t, b: a[:, 4 * b:4 * b + 4, t * P:(t + 1) * P]
                in_bank = lambda b: bank[b][:, :].rearrange("p (k s) -> p k s", k=4)
                with nc.Block() as block:
                    @block.gpsimd
                    def _(pool):
                        for t in range(TT):
                            for g in range(2):
                                nc.gpsimd.indirect_dma_start(rows[:, 2 * t + g, :], None, y_dram[l],
                                                             bass.IndirectOffsetOnAxis(ap=slots[:, t, g:g + 1], axis=0)
                                                             ).then_inc(fetched[t], 16)
                        later_pool(pool)
                        add_biases(pool, ln_b, in_ln, scaled, normed)

                    @block.sync
                    def _(sp):
                        sp.wait_ge(fetched[0], 32)
                        for row, dst in ((ln2_g, ln_g), (ln2_b, ln_b)):
                            sp.dma_start(dst[:, :], row[l].unsqueeze(0).broadcast_to([P, D_MODEL])).then_inc(in_ln, 16)
                        later_sp(sp)
                        if not last_layer:
                            for t in range(TT):
                                sp.wait_ge(fetched[t], 32)
                            load_mlstm_slab(sp, 0)
                            load_mlstm_slab(sp, 1)
                        if last_layer:
                            for t in range(TT):
                                sp.wait_ge(normed, t + 1)
                                sp.dma_start(out[0].rearrange("(t p) d -> p t d", t=TT)[:, t, :],
                                             x_sb[:, t, :]).then_inc(stored, 16)
                            sp.wait_ge(stored, 16 * TT)

                    @block.vector
                    def _(dve):
                        dve_chain.bind(dve)
                        later_dve(dve)
                        then = dve_chain.then

                        def trailing(t):
                            for b in range(2):
                                dve.wait_ge(copied, 2 * t + b + 1)
                                nc.vector.tensor_tensor(by_tile(x2_half[1], t, b), in_bank(b), by_tile(x2_half[0], t, b),
                                                        ALU.subtract).then_inc(lo_ready, 1)

                        def combine(t):
                            dve.wait_ge(fetched[t], 32)
                            xt, a, b = x_sb[:, t, :], rows[:, 2 * t, :], rows[:, 2 * t + 1, :]
                            dve.wait_ge(first_gated, t + 1)
                            then(nc.vector.scalar_tensor_tensor(a, b, gates[:, t, 1:2], a, ALU.mult, ALU.add))
                            then(nc.vector.scalar_tensor_tensor(xt, xt, ALPHA, a, ALU.mult, ALU.add))
                            moments(t, var_ready)

                        def invert(t):
                            m = mv[:, t, :]
                            dve.wait_ge(std_ready, t + 1)
                            then(nc.vector.reciprocal(m[:, 2:3], m[:, 3:4]))
                            nc.vector.scalar_tensor_tensor(m[:, 3:4], m[:, 0:1], -1.0, m[:, 2:3], ALU.mult,
                                                           ALU.mult).then_inc(inverted, 1)

                        def scale(t):
                            dve.wait_ge(normalized, t + 1)
                            scale_and_shift(dve, t, ln_g, ln_b, scaled, normed)

                        for t in range(TT):
                            combine(t)
                            if t == 1:
                                dve.wait_ge(in_ln, 32)
                            if t:
                                scale(t - 1)
                            invert(t)
                            if t >= 2 and not last_layer:
                                trailing(t - 2)
                        scale(TT - 1)
                        if not last_layer:
                            trailing(TT - 2)
                            trailing(TT - 1)

                    @block.tensor
                    def _(pe):
                        later_pe(pe)
                        if not last_layer:
                            for t in range(TT):
                                pe.wait_ge(normed, t + 1)
                                for b in range(2):
                                    if t:
                                        pe.wait_ge(lo_ready, 2 * t - 1 + b)
                                    for j in range(4):
                                        k = 4 * b + j
                                        last = nc.tensor.transpose(bank[b][:, j * P:(j + 1) * P],
                                                                   x_sb[:, t, k * P:(k + 1) * P], ident[:, :])
                                    last.then_inc(turned, 1)

                    @block.scalar
                    def _(act):
                        def gate_first(t):
                            act.wait_ge(fetched[t], 32)
                            nc.scalar.mul(rows[:, 2 * t, :], rows[:, 2 * t, :], gates[:, t, 0:1]).then_inc(first_gated, 1)

                        def leading(t):
                            for b in range(2):
                                act.wait_ge(turned, 2 * t + b + 1)
                                nc.scalar.copy(by_tile(x2_half[0], t, b), in_bank(b)).then_inc(copied, 1)

                        later_act(act)
                        gate_first(0)
                        for t in range(TT):
                            if t + 1 < TT:
                                gate_first(t + 1)
                            std_of_tile(act, t, var_ready, std_ready)
                            act.wait_ge(inverted, t + 1)
                            nc.scalar.activation(x_sb[:, t, :], x_sb[:, t, :], ACT.Identity, bias=mv[:, t, 3:4],
                                                 scale=mv[:, t, 2:3]).then_inc(normalized, 1)
                            if t and not last_layer:
                                leading(t - 1)
                        if not last_layer:
                            leading(TT - 1)


        def mlstm_phase():
            ph = ExitStack()
            ph.callback(end_phase)
            HD = ML_DH + 1
            with ph:
                s = lambda n: sem("p4_" + n, ph)
                places = [ring_at + 4 * o for o in (8192, 10240, 2 * W_EXP + 4096, 2 * W_EXP + 6144)]
                w_half = [halves_at(f"w1_half{i}", [P, KT * P], at, at + 4096) for i, at in enumerate(places)]
                take = lambda o, n: R1[:, o:o + n]
                qT = take(0, 3072).rearrange("p (h s) -> p h s", h=ML_HEADS)
                kT = take(3072, 3072).rearrange("p (h s) -> p h s", h=ML_HEADS)
                v_aug = take(6144, TT * ML_HEADS * HD).rearrange("p (t h d) -> p t h d", t=TT, h=ML_HEADS)
                probs = take(9240, 1024).rearrange("p (t m) -> p t m", t=TT)
                probsT = take(10264, 1024).rearrange("p (m t) -> p m t", m=MT)
                top_row, total_row = R1[0:ML_HEADS, 11288:11800], sb("top_next", [ML_HEADS, 1 + 2 * N_CHUNKS], at=ph)
                ogate = sb("ogate", [P, TT, MIX_W], at=ph)
                qmT = sb("qmT1", [P, 2, SEQ], at=ph)
                row_sel = sb("row_sel", [ML_HEADS, ML_HEADS, P], at=ph)
                cols = sb("cols", [P, N_CHUNKS, P], at=ph)
                vec = (sb("att_top1", [P, 8], at=ph), sb("att_sum1", [P, 4], at=ph), sb("att_inv1", [P, 4], at=ph))
                row = lambda i: headsT[0:ML_HEADS, i, :]
                in_gate, log_f, b_row, t_row, decay_out = row(0), row(1), row(2), row(3), headsT[:, 5, :]
                flat = xT[:, :, :].rearrange("p k s -> p (k s)")
                cell = lambda i, n: flat[:, i * 784:i * 784 + ML_HEADS * n].rearrange("p (h d) -> p h d", h=ML_HEADS)
                ex, S, kw, qC, state = cell(0, P), cell(1, P), cell(2, P), cell(3, HD), cell(4, HD)
                hh = qmT[:, :, :].rearrange("p j s -> p (j s)")[:, 0:ML_HEADS * P].rearrange("p (h d) -> p h d", h=ML_HEADS)
                den = sb("den", [P, ML_HEADS], at=ph)
                stat6, mv6 = sb("stat6", [P, ML_HEADS, 6], at=ph), sb("mv6", [P, ML_HEADS, 2], at=ph)
                std6 = sb("std6", [P, ML_HEADS], at=ph)
                decay = sb("decay", [P, ML_HEADS, N_CHUNKS], at=ph)

                consts, cols_read = s("consts"), s("cols_read")
                w_hi_ready, w_lo_ready = s("w_hi"), s("w_lo")
                projected, by_act, by_dve = s("projected"), s("by_act"), s("by_dve")
                g_abs, g_exp, b_ready, m_ready = s("g_abs"), s("g_exp"), s("b_ready"), s("m_ready")
                rows_ready, cols_turned = s("rows_ready"), s("cols_turned")
                att = Attention("b", ph, qmT, kmT, vm, probs, probsT, vec)

                script = [("gates", 0), ("qm", 0), ("qm", 1), ("S", 0)]
                script += [("q", h) for h in range(4)] + [("T", 0), ("S", 1)] + [("q", 4), ("q", 5), ("k", 0)]
                script += [("V", 0), ("T", 1), ("S", 2)] + [("k", h) for h in (1, 2, 3)] + [("V", 1), ("T", 2), ("S", 3)]
                script += [("k", 4), ("k", 5), ("V", 2), ("T", 3), ("wide", 0), ("wide", 1), ("V", 3), ("cols", 0)]
                script += [("wide", i) for i in range(2, 12)]
                pieces = [st for st in script if st[0] not in ("S", "T", "V", "cols")]
                split_script = [("W", i) for i in range(3)]
                for st in script:
                    if st in pieces and pieces.index(st) + 3 < len(pieces):
                        split_script.append(("W", pieces.index(st) + 3))
                    split_script.append(st)

                def slab_of(i):
                    kind, n = pieces[i]
                    if kind in ("gates", "qm"):
                        return 0
                    return 4 + n // 4 if kind == "wide" else 1 + (n + (6 if kind == "k" else 0)) // 4

                results, ends = [], []
                for i, (kind, n) in enumerate(pieces):
                    if kind != "wide":
                        results.append((kind, n, 2 + i % 3, kind != "gates"))
                        ends.append((ends[-1] if ends else 0) + 1)
                    elif n % 4 < 3:
                        ends.append(ends[-1] + 1)
                    else:
                        banks = ((2, 3, 4, 6), (0, 1, 5, 7), (2, 3, 4, 6))[n // 4]
                        results += [(("v", "vo", "o")[n // 4], t, banks[t], n // 4 > 0) for t in range(TT)]
                        ends.append(ends[-1] + TT)

                def ended(m):
                    what, n = results[m][0:2]
                    if what in ("v", "vo", "o"):
                        return ends[pieces.index(("wide", 4 * ("v", "vo", "o").index(what) + 3))] - TT + n + 1
                    return ends[pieces.index((what, n))]

                def read_out(eng, m):
                    by = results[m][3]
                    eng.wait_ge(by_act if by else by_dve, sum(z[3] == by for z in results[:m + 1]))

                def bank_free(eng, m):
                    for q in range(m - 1, -1, -1):
                        if results[q][2] == results[m][2]:
                            return read_out(eng, q)

                def raw_weights(eng, i):
                    (kind, n), j = pieces[i], slab_of(i)
                    eng.wait_ge(in_w[j % 2], 16 * (j // 2 + 1))
                    w = slab[j % 2]
                    whole = lambda a: a[:, :].rearrange("p (k n) -> p k n", k=KT)
                    if kind == "gates":
                        return [(w[:, :, g * ML_HEADS:(g + 1) * ML_HEADS],
                                 lambda a, g=g: whole(a)[:, :, 32 * g:32 * g + ML_HEADS]) for g in range(2)]
                    if kind == "wide":
                        return [(w[:, n % 4 * 2:n % 4 * 2 + 2, :], lambda a: a[:, :].rearrange("p (k n) -> p k n", k=2))]
                    c = 2 * ML_HEADS + n * P if kind == "qm" else (n + (6 if kind == "k" else 0)) % 4 * P
                    return [(w[:, :, c:c + P], whole)]

                with nc.Block() as block:
                    @block.gpsimd
                    def _(pool):
                        pool_chain.bind(pool)
                        then = pool_chain.then
                        nc.gpsimd.memset(w_half[0][0][:, :].rearrange("p (k n) -> p k n", k=KT)[:, :, ML_HEADS:32].bitcast(F32), 0.0)
                        nc.gpsimd.memset(w_half[0][1][:, :].rearrange("p (k n) -> p k n", k=KT)[:, :, ML_HEADS:32].bitcast(F32),
                                         0.0).then_inc(consts, 1)
                        then(nc.gpsimd.memset(row_sel[:, :, :], 0.0))
                        then(nc.gpsimd.affine_select(out=row_sel[:, :, :], in_=row_sel[:, :, :], compare_op=ALU.not_equal,
                                                     fill=1.0, base=0, pattern=[[-1, ML_HEADS], [0, P]], channel_multiplier=1))
                        then(nc.gpsimd.memset(v_aug[:, :, :, ML_DH:HD], 1.0))
                        nc.gpsimd.memset(decay_out[:, :], 0.0).then_inc(consts, 1)

                    @block.sync
                    def _(sp):
                        for i in range(2, len(slabs)):
                            sp.wait_ge(w_lo_ready, max(j for j in range(len(pieces)) if slab_of(j) == i - 2) + 1)
                            load_mlstm_slab(sp, i)

                    @block.tensor
                    def _(pe):
                        x_hi, x_lo = x2_half
                        i = m = 0
                        for kind, n in script:
                            if kind in ("S", "T", "V"):
                                if (kind, n) == ("S", 0):
                                    read_out(pe, 2)
                                att.pe(pe, kind, n)
                                continue
                            if kind == "cols":
                                pe.wait_ge(rows_ready, 1)
                                pe.wait_ge(att.out, 4)
                                for c in range(N_CHUNKS):
                                    nc.tensor.transpose(bank[7][:, c * P:(c + 1) * P], decay_out[:, c * P:(c + 1) * P], ident[:, :])
                                for h in range(ML_HEADS):
                                    last = nc.tensor.matmul(bank[5][:, h * N_CHUNKS:(h + 1) * N_CHUNKS], row_sel[:, h, :],
                                                            decay_out[0:ML_HEADS, P - 1::P], start=True, stop=True)
                                last.then_inc(cols_turned, 1)
                                continue
                            pe.wait_ge(w_lo_ready, i + 1)
                            if kind == "gates":
                                pe.wait_ge(consts, 2)
                            if kind != "wide":
                                bank_free(pe, m)
                                cols_of = 32 + ML_HEADS if kind == "gates" else P
                                hi, lo = (a[:, :].rearrange("p (k n) -> p k n", k=KT) for a in w_half[i % 4])
                                for k in range(KT):
                                    for w, xh in ((hi, x_hi), (hi, x_lo), (lo, x_hi)):
                                        last = nc.tensor.matmul(bank[results[m][2]][0:cols_of, :], w[:, k, 0:cols_of], xh[:, k, :],
                                                                start=(k == 0 and w is hi and xh is x_hi),
                                                                stop=(k == KT - 1 and w is lo))
                                last.then_inc(projected, 1)
                                m += 1
                            else:
                                hi, lo = (a[:, :].rearrange("p (k n) -> p k n", k=2) for a in w_half[i % 4])
                                if n == 4:
                                    pe.wait_ge(cols_read, 1)
                                for t in range(TT):
                                    if n % 4 == 0:
                                        bank_free(pe, m + t)
                                    z = slice(t * P, (t + 1) * P)
                                    for k in range(2):
                                        kk = n % 4 * 2 + k
                                        for w, xh in ((hi, x_hi), (hi, x_lo), (lo, x_hi)):
                                            last = nc.tensor.matmul(bank[results[m + t][2]][:, :], xh[:, kk, z], w[:, k, :],
                                                                    start=(kk == 0 and w is hi and xh is x_hi),
                                                                    stop=(kk == KT - 1 and w is lo))
                                    if n % 4 == 3:
                                        last.then_inc(projected, 1)
                                if n % 4 < 3:
                                    last.then_inc(projected, 1)
                                else:
                                    m += TT
                            i += 1

                    @block.scalar
                    def _(act):
                        act_chain.bind(act)
                        then = act_chain.then

                        def take_out(m):
                            what, n, b, _ = results[m]
                            if what == "gates":
                                act.wait_ge(g_abs, 1)
                                then(nc.scalar.activation(t_row, t_row, ACT.Exp, scale=-1.0))
                                nc.scalar.activation(t_row, t_row, ACT.Ln, bias=1.0).then_inc(g_exp, 1)
                            elif what != "v":
                                o = bank[b]
                                act.wait_ge(projected, ended(m))
                                if what == "qm":
                                    ins = nc.scalar.copy(qmT[:, n, :], o[:, :])
                                elif what == "q":
                                    ins = nc.scalar.copy(qT[:, n, :], o[:, :])
                                elif what == "k":
                                    ins = nc.scalar.mul(kT[:, n, :], o[:, :], ML_DH ** -0.5)
                                elif what == "vo":
                                    nc.scalar.copy(v_aug[:, n, 4:6, 0:ML_DH], o[:, 0:256].rearrange("p (h d) -> p h d", h=2))
                                    ins = nc.scalar.activation(ogate[:, n, 0:256], o[:, 256:512], ACT.Sigmoid)
                                else:
                                    ins = nc.scalar.activation(ogate[:, n, 256:768], o[:, :], ACT.Sigmoid)
                                ins.then_inc(by_act, 1)

                        def gate_rows():
                            act.wait_ge(m_ready, 1)
                            for c in range(N_CHUNKS):
                                z = slice(c * P, (c + 1) * P)
                                nc.scalar.activation(decay_out[0:ML_HEADS, z], top_row[:, z], ACT.Exp,
                                                     bias=total_row[:, c:c + 1], scale=-1.0)
                                nc.scalar.activation(decay_out[96:96 + ML_HEADS, z], in_gate[:, z], ACT.Exp,
                                                     bias=total_row[:, N_CHUNKS + 1 + c:N_CHUNKS + 2 + c])
                            nc.scalar.activation(decay_out[64:64 + ML_HEADS, :], b_row, ACT.Exp, scale=-1.0).then_inc(rows_ready, 1)

                        m = 0
                        for st in split_script:
                            kind = st[0]
                            if kind in ("S", "T", "V"):
                                att.act(act, kind, st[1])
                                if st == ("S", 0):
                                    gate_rows()
                            elif kind == "cols":
                                continue
                            elif kind == "W":
                                i = st[1]
                                raw = raw_weights(act, i)
                                if i == 0:
                                    act.wait_ge(consts, 1)
                                if i >= 4:
                                    act.wait_ge(projected, ends[i - 4])
                                for part, of in raw:
                                    last = nc.scalar.copy(of(w_half[i % 4][0]), part)
                                last.then_inc(w_hi_ready, 1)
                            elif kind != "wide" or st[1] % 4 == 3:
                                for _ in range(TT if kind == "wide" else 1):
                                    take_out(m)
                                    m += 1

                    @block.vector
                    def _(dve):
                        dve_chain.bind(dve)
                        then = dve_chain.then
                        V = nc.vector
                        m = 0
                        dve.wait_ge(consts, 1)
                        for st in split_script:
                            kind = st[0]
                            if kind in ("S", "T", "V"):
                                att.dve(dve, kind, st[1])
                            elif kind == "cols":
                                dve.wait_ge(cols_turned, 1)
                                V.tensor_copy(cols[:, :, :].rearrange("p c x -> p (c x)"), bank[7][:, :])
                                V.tensor_copy(decay[:, :, :].rearrange("p h c -> p (h c)"),
                                              bank[5][:, 0:ML_HEADS * N_CHUNKS]).then_inc(cols_read, 1)
                            elif kind == "W":
                                i = st[1]
                                raw, (hi, lo) = raw_weights(dve, i), w_half[i % 4]
                                dve.wait_ge(w_hi_ready, i + 1)
                                for part, of in raw:
                                    last = V.tensor_tensor(of(lo), part, of(hi), ALU.subtract)
                                last.then_inc(w_lo_ready, 1)
                            elif kind == "gates":
                                dve.wait_ge(consts, 2)
                                o = bank[results[m][2]]
                                m += 1
                                dve.wait_ge(projected, 1)
                                V.tensor_scalar(in_gate, o[0:ML_HEADS, :], gate_bias[0:ML_HEADS, :], None, ALU.add)
                                ins = V.tensor_scalar(log_f, o[32:32 + ML_HEADS, :], gate_bias[32:32 + ML_HEADS, :], None, ALU.add)
                                ins.then_inc(by_dve, 1)
                                dve.wait_ge(by_dve, 1)
                                V.scalar_tensor_tensor(t_row, log_f, -1.0, log_f, ALU.mult, ALU.max).then_inc(g_abs, 1)
                                dve.wait_ge(g_exp, 1)
                                then(V.scalar_tensor_tensor(log_f, log_f, 0.0, t_row, ALU.min, ALU.subtract))
                                then(V.memset(t_row, 1.0))
                                then(V.memset(total_row[:, 0:1], 0.0))
                                for c in range(N_CHUNKS):
                                    z = slice(c * P, (c + 1) * P)
                                    then(V.tensor_tensor_scan(b_row[:, z], t_row[:, z], log_f[:, z], 0.0, ALU.mult, ALU.add))
                                then(V.tensor_tensor(in_gate, in_gate, b_row, ALU.subtract))
                                for c in range(N_CHUNKS):
                                    z = slice(c * P, (c + 1) * P)
                                    at_last = slice((c + 1) * P - 1, (c + 1) * P)
                                    then(V.tensor_tensor_scan(top_row[:, z], in_gate[:, z], in_gate[:, z],
                                                              total_row[:, c:c + 1], ALU.max, ALU.max))
                                    if c < N_CHUNKS - 1:
                                        then(V.tensor_tensor(total_row[:, c + 1:c + 2], top_row[:, at_last], b_row[:, at_last],
                                                             ALU.add))
                                    then(V.tensor_scalar(total_row[:, N_CHUNKS + 1 + c:N_CHUNKS + 2 + c], top_row[:, at_last],
                                                         -1.0, None, ALU.mult))
                                then(V.tensor_copy(decay_out[32:32 + ML_HEADS, :], in_gate))
                                V.tensor_tensor(b_row, b_row, top_row, ALU.add).then_inc(m_ready, 1)
                            elif kind != "wide":
                                m += 1
                            elif st[1] == 3:
                                for t in range(TT):
                                    dve.wait_ge(projected, ended(m))
                                    V.tensor_copy(v_aug[:, t, 0:4, 0:ML_DH],
                                                  bank[results[m][2]][:, :].rearrange("p (h d) -> p h d", h=4)).then_inc(by_dve, 1)
                                    m += 1

                cell_phase(ph, locals_of=dict(qT=qT, kT=kT, v_aug=v_aug, ogate=ogate, row_sel=row_sel, cols=cols, top_row=top_row,
                                              ex=ex, S=S, kw=kw, qC=qC, state=state, den=den, stat6=stat6, mv6=mv6, std6=std6,
                                              decay=decay, hh=hh))

        def cell_phase(ph, locals_of):
            d = locals_of
            qT, kT, v_aug, ogate, row_sel, cols, top_row = (d[n] for n in ("qT", "kT", "v_aug", "ogate", "row_sel", "cols", "top_row"))
            ex, S, kw, qC, state, den = (d[n] for n in ("ex", "S", "kw", "qC", "state", "den"))
            stat6, mv6, std6, decay, hh = (d[n] for n in ("stat6", "mv6", "std6", "decay", "hh"))
            HD = ML_DH + 1
            s = lambda n: sem("p5_" + n, ph)
            spread, compared, exped, weighed = s("spread"), s("compared"), s("exped"), s("weighed")
            k_turned, k_weighed, inter, intra, added = s("k_turned"), s("k_weighed"), s("inter"), s("intra"), s("added")
            updated, state_ready, var6, std_done = s("updated"), s("state_ready"), s("var6"), s("std_done")
            h_ready, h_turned, h_out, inter_read = s("h_ready"), s("h_turned"), s("h_out"), s("inter_read")
            scored = s("scored")
            pair = lambda b, w: [bank[b + i][:, 0:3 * w].rearrange("p (h d) -> p h d", h=3) for i in range(2)]
            W_COL, C_COL, EM_COL, WS_COL = 0, 32, 64, 96
            with nc.Block() as block:
                @block.sync
                def _(sp):
                    sp.dma_start(w_out_sb, w_out[1].rearrange("(k p) n -> p k n", p=P)).then_inc(in_w_out[1], 16)

                @block.tensor
                def _(pe):
                    def front(c):
                        z = slice(c * P, (c + 1) * P)
                        if c:
                            pe.wait_ge(k_weighed, c)
                        for h in range(ML_HEADS):
                            last = nc.tensor.matmul(pair(0, P)[h // 3][:, h % 3, :], row_sel[:, h, :], top_row[:, z],
                                                    start=True, stop=True)
                        last.then_inc(spread, 1)
                        if c:
                            pe.wait_ge(state_ready, c)
                        for h in range(ML_HEADS):
                            last = nc.tensor.matmul(pair(2, P)[h // 3][:, h % 3, :], kT[:, h, z], qT[:, h, z], start=True, stop=True)
                        last.then_inc(scored, 1)
                        if c < N_CHUNKS - 1:
                            pe.wait_ge(compared, c + 1)
                            for h in range(ML_HEADS):
                                last = nc.tensor.transpose(pair(0, P)[h // 3][:, h % 3, :], kT[:, h, z], ident[:, :])
                            last.then_inc(k_turned, 1)

                    def turn_out(c):
                        pe.wait_ge(h_ready, c + 1)
                        if c < N_CHUNKS - 1:
                            pe.wait_ge(inter_read, c + 1)
                        else:
                            pe.wait_ge(h_out, 2 * c)
                        for h in range(ML_HEADS):
                            last = nc.tensor.transpose(pair(6, P)[h // 3][:, h % 3, :], hh[:, h, :], ident[:, :])
                        last.then_inc(h_turned, 1)

                    front(0)
                    for c in range(N_CHUNKS):
                        z = slice(c * P, (c + 1) * P)
                        if c:
                            if c > 1:
                                pe.wait_ge(h_out, 2 * (c - 1))
                            pe.wait_ge(state_ready, c)
                            for h in range(ML_HEADS):
                                last = nc.tensor.matmul(pair(6, HD)[h // 3][:, h % 3, :], qT[:, h, z], state[:, h, :],
                                                        start=True, stop=True)
                            last.then_inc(inter, 1)
                        pe.wait_ge(weighed, c + 1)
                        if c:
                            pe.wait_ge(added, c)
                        for h in range(ML_HEADS):
                            last = nc.tensor.matmul(pair(4, HD)[h // 3][:, h % 3, :], S[:, h, :], v_aug[:, c, h, :],
                                                    start=True, stop=True)
                        last.then_inc(intra, 1)
                        if c < N_CHUNKS - 1:
                            pe.wait_ge(k_weighed, c + 1)
                            for h in range(ML_HEADS):
                                last = nc.tensor.matmul(pair(2, HD)[h // 3][:, h % 3, :], kw[:, h, :], v_aug[:, c, h, :],
                                                        start=True, stop=True)
                            last.then_inc(updated, 1)
                        if c < N_CHUNKS - 1:
                            front(c + 1)
                        if c:
                            turn_out(c - 1)
                    turn_out(N_CHUNKS - 1)

                @block.scalar
                def _(act):
                    def write_out(c):
                        act.wait_ge(h_turned, c + 1)
                        for i in range(2):
                            for j in range(3):
                                h = 3 * i + j
                                last = nc.scalar.mul(headsT[:, h, c * P:(c + 1) * P], pair(6, P)[i][:, j, :], norm_g_sb[:, h:h + 1])
                            last.then_inc(h_out, 1)

                    def weights(c):
                        act.wait_ge(compared, c + 1)
                        nc.scalar.activation(ex[:, :, :], ex[:, :, :], ACT.Exp, scale=-1.0).then_inc(exped, 1)

                    weights(0)
                    for c in range(N_CHUNKS):
                        if c < N_CHUNKS - 1:
                            weights(c + 1)
                        if c:
                            write_out(c - 1)
                        act.wait_ge(var6, c + 1)
                        nc.scalar.activation(std6[:, :], mv6[:, :, 1], ACT.Sqrt, bias=eps_col[:, :]).then_inc(std_done, 1)
                    write_out(N_CHUNKS - 1)

                @block.vector
                def _(dve):
                    dve_chain.bind(dve)
                    then = dve_chain.then
                    V = nc.vector
                    three = lambda a, i: a[:, 3 * i:3 * i + 3, :]
                    col = lambda c, kind, i, w: cols[:, c, kind + 3 * i:kind + 3 * i + 3].unsqueeze(2).broadcast_to([P, 3, w])

                    def compare(c):
                        dve.wait_ge(spread, c + 1)
                        if c:
                            dve.wait_ge(weighed, c)
                        for h in range(ML_HEADS):
                            last = V.scalar_tensor_tensor(ex[:, h, :], pair(0, P)[h // 3][:, h % 3, :],
                                                          cols[:, c, C_COL + h:C_COL + h + 1], future_big[:, :],
                                                          ALU.subtract, ALU.max)
                        last.then_inc(compared, 1)

                    def weigh_keys(c):
                        dve.wait_ge(k_turned, c + 1)
                        if c:
                            dve.wait_ge(updated, c)
                        for i in range(2):
                            last = V.tensor_tensor(three(kw, i), pair(0, P)[i], col(c, WS_COL, i, P), ALU.mult)
                        last.then_inc(k_weighed, 1)

                    def weigh_scores(c):
                        dve.wait_ge(exped, c + 1)
                        dve.wait_ge(scored, c + 1)
                        if c:
                            dve.wait_ge(intra, c)
                        for i in range(2):
                            last = V.tensor_tensor(three(S, i), pair(2, P)[i], three(ex, i), ALU.mult)
                        last.then_inc(weighed, 1)

                    def sums_and_state(c):
                        if c:
                            dve.wait_ge(inter, c)
                            for i in range(2):
                                last = V.tensor_tensor(three(qC, i), pair(6, HD)[i], col(c, W_COL, i, HD), ALU.mult)
                            last.then_inc(inter_read, 1)
                            dve.wait_ge(inter_read, c)
                        dve.wait_ge(intra, c + 1)
                        for i in range(2):
                            if c:
                                last = V.tensor_tensor(three(qC, i), pair(4, HD)[i], three(qC, i), ALU.add)
                            else:
                                last = V.tensor_copy(three(qC, i), pair(4, HD)[i])
                        last.then_inc(added, 1)
                        dve.wait_ge(added, c + 1)
                        if c < N_CHUNKS - 1:
                            dve.wait_ge(updated, c + 1)
                            for h in range(ML_HEADS):
                                new = pair(2, HD)[h // 3][:, h % 3, :]
                                if c:
                                    last = V.scalar_tensor_tensor(state[:, h, :], state[:, h, :], decay[:, h, c:c + 1], new,
                                                                  ALU.mult, ALU.add)
                                else:
                                    last = V.tensor_copy(state[:, h, :], new)
                            last.then_inc(state_ready, 1)

                    def divide(c):
                        dcol = qC[:, :, ML_DH]
                        then(V.scalar_tensor_tensor(den[:, :], dcol, -1.0, dcol, ALU.mult, ALU.max))
                        then(V.tensor_tensor(den[:, :], den[:, :], cols[:, c, EM_COL:EM_COL + ML_HEADS], ALU.max))
                        then(V.reciprocal(den[:, :], den[:, :]))
                        if c:
                            dve.wait_ge(h_turned, c)
                        then(V.tensor_tensor(hh[:, :, :], qC[:, :, 0:ML_DH], den[:, :].unsqueeze(2).broadcast_to([P, ML_HEADS, ML_DH]),
                                             ALU.mult))
                        for h in range(ML_HEADS):
                            last = V.bn_stats(stat6[:, h, :], hh[:, h, :])
                        then(last)
                        for h in range(ML_HEADS):
                            last = V.bn_aggr(mv6[:, h, :], stat6[:, h, :])
                        last.then_inc(var6, 1)

                    def norm(c):
                        dve.wait_ge(std_done, c + 1)
                        then(V.reciprocal(std6[:, :], std6[:, :]))
                        for h in range(ML_HEADS):
                            last = V.tensor_scalar(hh[:, h, :], hh[:, h, :], mv6[:, h, 0:1], std6[:, h:h + 1], ALU.subtract, ALU.mult)
                        then(last)
                        V.tensor_tensor(hh[:, :, :], hh[:, :, :], ogate[:, c, :].rearrange("p (h d) -> p h d", h=ML_HEADS),
                                        ALU.mult).then_inc(h_ready, 1)

                    compare(0)
                    weigh_keys(0)
                    weigh_scores(0)
                    for c in range(N_CHUNKS):
                        sums_and_state(c)
                        if c < N_CHUNKS - 1:
                            compare(c + 1)
                        if c:
                            norm(c - 1)
                        if c < N_CHUNKS - 2:
                            weigh_keys(c + 1)
                        if c < N_CHUNKS - 1:
                            weigh_scores(c + 1)
                        divide(c)
                    norm(N_CHUNKS - 1)

        def dump():
            done = sem("dumped")
            with nc.Block() as block:
                @block.sync
                def _(sp):
                    sp.dma_start(out[0].rearrange("(t p) d -> p t d", t=TT), x_sb[:, :, :]).then_inc(done, 16)
                    sp.wait_ge(done, 16)
        conv_phase()
        route = ExitStack()
        mem_l = route_memory(0, route)
        out_and_route_phase(0, mem_l)
        if stop == 1:
            return dump()
        expert_phase(0, mem_l)
        route.close()
        combine_phase(0)
        if stop == 3:
            return dump()
        mlstm_phase()
        route = ExitStack()
        mem_l = route_memory(1, route)
        out_and_route_phase(1, mem_l)
        if stop == 5:
            return dump()
        expert_phase(1, mem_l)
        route.close()
        combine_phase(1)


_INS = ['x', 'mem', 'conv_w_in', 'conv_w', 'mlstm_w_in', 'mlstm_gate_b', 'mlstm_norm_g', 'w_kv_mem', 'w_out',
        'ln1_g', 'ln1_b', 'ln2_g', 'ln2_b', 'router_w', 'router_b', 'w_gate', 'w_up', 'w_down']


def kernel(**inputs):
    import numpy as _np
    import concourse.bacc as _bacc
    from concourse.bass_utils import run_bass_kernel_spmd as _run

    nc = _bacc.Bacc("TRN2", target_bir_lowering=False, num_devices=1)
    arrays, args = {}, []
    for name in _INS:
        a = _np.ascontiguousarray(inputs[name])
        arrays[f"in_{name}"] = a
        args.append(nc.dram_tensor(f"in_{name}", a.shape, mybir.dt.from_np(a.dtype), kind="ExternalInput").ap())
    out = nc.dram_tensor("out", (1, SEQ, D_MODEL), F32, kind="ExternalOutput").ap()
    build_trunk(nc, *args, out)
    r = _run(nc, [arrays], core_ids=[0])
    return r.results[0]["out"]
```
